# Optimizing a Trainium2 kernel written in Bass

```python
import math
import jax, jax.numpy as jnp
from jax import lax
import numpy as np

D_MODEL = 2048
BATCH = 1
SEQ = 256
DEPTH = 1
DEC_BATCH = 8
DEC_SEQ = 16
PAST_LEN = 128

CHUNK = 64
N_META = 16
D_CONV = D_MODEL // 2
CONV_W = 3
D_SSM = D_MODEL // 2
SSM_H = 16
SSM_G = D_SSM // SSM_H
SSM_P = 64
N_EGROUPS = 4
EXPERTS_PER_GROUP = 8
N_EXPERTS = N_EGROUPS * EXPERTS_PER_GROUP
TOP_K_IN_GROUP = 2
D_EXPERT = D_MODEL // 8
EPS = 1e-6
D_IN = 3 * D_CONV + D_SSM + 2 * D_MODEL
DT_MIN = 1e-3
DT_MAX = 1e-1

kernel_name = "gated_conv_s5_hmoe_stream_step"

def rmsnorm(x, g):
    xf = x.astype(jnp.float32)
    xf = xf * lax.rsqrt(jnp.mean(xf * xf, axis=-1, keepdims=True) + EPS)
    return (xf * g.astype(jnp.float32)).astype(x.dtype)

def short_conv(z, buf, w):
    L = z.shape[1]
    zp = jnp.concatenate([buf.astype(z.dtype), z], axis=1)
    y = w[0] * zp[:, 0:L]
    for k in range(1, CONV_W):
        y = y + w[k] * zp[:, k:k + L]
    return y, zp[:, -(CONV_W - 1):]

def s5_discretize(lam_re, lam_im, log_dt, b_re, b_im):
    f32 = jnp.float32
    dt = jnp.exp(log_dt.astype(f32))[:, None]
    lr, li = lam_re.astype(f32), lam_im.astype(f32)
    mag = jnp.exp(lr * dt)
    ab_re, ab_im = mag * jnp.cos(li * dt), mag * jnp.sin(li * dt)
    nr, ni = ab_re - 1.0, ab_im
    den = lr * lr + li * li
    k_re = (nr * lr + ni * li) / den
    k_im = (ni * lr - nr * li) / den
    br, bi = b_re.astype(f32), b_im.astype(f32)
    bb_re = k_re[..., None] * br - k_im[..., None] * bi
    bb_im = k_re[..., None] * bi + k_im[..., None] * br
    return ab_re, ab_im, bb_re, bb_im

def _scan_combine(e1, e2):
    a1r, a1i, b1r, b1i = e1
    a2r, a2i, b2r, b2i = e2
    ar = a2r * a1r - a2i * a1i
    ai = a2r * a1i + a2i * a1r
    br = a2r * b1r - a2i * b1i + b2r
    bi = a2r * b1i + a2i * b1r + b2i
    return ar, ai, br, bi

def s5_scan(u, s0_re, s0_im, ab_re, ab_im, bb_re, bb_im):
    bu_re = jnp.einsum('gph,blgh->blgp', bb_re, u)
    bu_im = jnp.einsum('gph,blgh->blgp', bb_im, u)
    s0r, s0i = s0_re.astype(jnp.float32), s0_im.astype(jnp.float32)
    bu_re = bu_re.at[:, 0].add(ab_re * s0r - ab_im * s0i)
    bu_im = bu_im.at[:, 0].add(ab_re * s0i + ab_im * s0r)
    a_re = jnp.broadcast_to(ab_re, bu_re.shape)
    a_im = jnp.broadcast_to(ab_im, bu_im.shape)
    _, _, s_re, s_im = lax.associative_scan(_scan_combine, (a_re, a_im, bu_re, bu_im), axis=1)
    return s_re, s_im

def hier_moe(v, w_coarse, w_fine, w_gate, w_up, w_down):
    bsz, L, D = v.shape
    t = v.reshape(-1, D)
    pc = jax.nn.softmax((t @ w_coarse).astype(jnp.float32), axis=-1)
    pg, gi = lax.top_k(pc, 1)
    lf = (t @ w_fine).astype(jnp.float32).reshape(-1, N_EGROUPS, EXPERTS_PER_GROUP)
    lf_g = jnp.take_along_axis(lf, gi[:, :, None], axis=1)[:, 0]
    vals, ei = lax.top_k(lf_g, TOP_K_IN_GROUP)
    wk = jax.nn.softmax(vals, axis=-1) * pg
    eid = gi * EXPERTS_PER_GROUP + ei
    gates = jnp.sum(jax.nn.one_hot(eid, N_EXPERTS, dtype=jnp.float32) * wk[..., None], axis=1)
    hg = jnp.einsum('td,edf->tef', t, w_gate)
    hu = jnp.einsum('td,edf->tef', t, w_up)
    act = jax.nn.silu(hg) * hu * gates[:, :, None].astype(t.dtype)
    out = jnp.einsum('tef,efd->td', act, w_down)
    return out.reshape(bsz, L, D)

def layer(h, conv_buf, s_re0, s_im0, lw):
    (norm1, w_in, conv_w, lam_re, lam_im, log_dt, b_re, b_im, c_re, c_im, d_skip,
     w_glu, w_conv_out, w_ssm_out, w_o, norm2, w_coarse, w_fine, w_gate, w_up, w_down) = lw
    bsz, L, _ = h.shape
    u = rmsnorm(h, norm1)
    p = u @ w_in
    xb, xc, xv, xs, ga, gb = jnp.split(
        p, [D_CONV, 2 * D_CONV, 3 * D_CONV, 3 * D_CONV + D_SSM, 3 * D_CONV + D_SSM + D_MODEL], axis=-1)
    yconv, new_buf = short_conv(xc * xv, conv_buf, conv_w)
    ya = (xb * yconv) @ w_conv_out
    us = xs.astype(jnp.float32).reshape(bsz, L, SSM_G, SSM_H)
    ab_re, ab_im, bb_re, bb_im = s5_discretize(lam_re, lam_im, log_dt, b_re, b_im)
    s_re, s_im = s5_scan(us, s_re0, s_im0, ab_re, ab_im, bb_re, bb_im)
    ys = (jnp.einsum('ghp,blgp->blgh', c_re.astype(jnp.float32), s_re)
          - jnp.einsum('ghp,blgp->blgh', c_im.astype(jnp.float32), s_im)
          + d_skip.astype(jnp.float32).reshape(SSM_G, SSM_H) * us)
    ys = jax.nn.gelu(ys.reshape(bsz, L, D_SSM).astype(h.dtype))
    ys = ys * jax.nn.sigmoid(ys @ w_glu)
    yb = ys @ w_ssm_out
    merged = jax.nn.sigmoid(ga) * ya + jax.nn.sigmoid(gb) * yb
    h = h + merged @ w_o
    h = h + hier_moe(rmsnorm(h, norm2), w_coarse, w_fine, w_gate, w_up, w_down)
    return h, new_buf, s_re[:, -1], s_im[:, -1]

def trunk(x, conv_state, ssm_re, ssm_im, stacked, final_norm):
    h = x
    new_conv, new_re, new_im = [], [], []
    for l in range(DEPTH):
        lw = tuple(w[l] for w in stacked)
        h, nb, nr, ni = layer(h, conv_state[l], ssm_re[l], ssm_im[l], lw)
        new_conv.append(nb)
        new_re.append(nr)
        new_im.append(ni)
    return rmsnorm(h, final_norm), jnp.stack(new_conv), jnp.stack(new_re), jnp.stack(new_im)

def setup_inputs(seed: int = 0) -> dict:
    key = jax.random.key(seed)
    ks = jax.random.split(key, 32)
    f32 = jnp.float32
    nrm = lambda k, shape, scale: jax.random.normal(k, shape, f32) * scale
    n_idx = jnp.arange(SSM_P, dtype=f32)
    log_dt = jax.random.uniform(ks[9], (DEPTH, SSM_G), f32, math.log(DT_MIN), math.log(DT_MAX))
    return {
        "x_prompt": nrm(ks[0], (BATCH, SEQ, D_MODEL), 1.0),
        "x_sample": nrm(ks[1], (DEC_BATCH, DEC_SEQ, D_MODEL), 1.0),
        "state_conv": nrm(ks[2], (DEPTH, DEC_BATCH, CONV_W - 1, D_CONV), 1.0),
        "state_ssm_re": nrm(ks[3], (DEPTH, DEC_BATCH, SSM_G, SSM_P), 0.1),
        "state_ssm_im": nrm(ks[4], (DEPTH, DEC_BATCH, SSM_G, SSM_P), 0.1),
        "meta_tokens": nrm(ks[5], (N_META, D_MODEL), 1.0),
        "norm1": 1.0 + nrm(ks[6], (DEPTH, D_MODEL), 0.02),
        "w_in": nrm(ks[7], (DEPTH, D_MODEL, D_IN), D_MODEL ** -0.5),
        "conv_w": nrm(ks[8], (DEPTH, CONV_W, D_CONV), CONV_W ** -0.5),
        "lam_re": -0.5 + nrm(ks[10], (DEPTH, SSM_G, SSM_P), 0.01),
        "lam_im": math.pi * n_idx + nrm(ks[11], (DEPTH, SSM_G, SSM_P), 0.01),
        "log_dt": log_dt,
        "ssm_b_re": nrm(ks[12], (DEPTH, SSM_G, SSM_P, SSM_H), (2 * SSM_H) ** -0.5),
        "ssm_b_im": nrm(ks[13], (DEPTH, SSM_G, SSM_P, SSM_H), (2 * SSM_H) ** -0.5),
        "ssm_c_re": nrm(ks[14], (DEPTH, SSM_G, SSM_H, SSM_P), (2 * SSM_P) ** -0.5),
        "ssm_c_im": nrm(ks[15], (DEPTH, SSM_G, SSM_H, SSM_P), (2 * SSM_P) ** -0.5),
        "ssm_d": nrm(ks[16], (DEPTH, D_SSM), 1.0),
        "w_glu": nrm(ks[17], (DEPTH, D_SSM, D_SSM), D_SSM ** -0.5),
        "w_conv_out": nrm(ks[18], (DEPTH, D_CONV, D_MODEL), D_CONV ** -0.5),
        "w_ssm_out": nrm(ks[19], (DEPTH, D_SSM, D_MODEL), D_SSM ** -0.5),
        "w_o": nrm(ks[20], (DEPTH, D_MODEL, D_MODEL), D_MODEL ** -0.5),
        "norm2": 1.0 + nrm(ks[21], (DEPTH, D_MODEL), 0.02),
        "w_coarse": nrm(ks[22], (DEPTH, D_MODEL, N_EGROUPS), D_MODEL ** -0.5),
        "w_fine": nrm(ks[23], (DEPTH, D_MODEL, N_EXPERTS), D_MODEL ** -0.5),
        "w_gate": nrm(ks[24], (DEPTH, N_EXPERTS, D_MODEL, D_EXPERT), D_MODEL ** -0.5),
        "w_up": nrm(ks[25], (DEPTH, N_EXPERTS, D_MODEL, D_EXPERT), D_MODEL ** -0.5),
        "w_down": nrm(ks[26], (DEPTH, N_EXPERTS, D_EXPERT, D_MODEL), D_EXPERT ** -0.5),
        "final_norm": 1.0 + nrm(ks[27], (D_MODEL,), 0.02),
    }

def reference(x_prompt, x_sample, state_conv, state_ssm_re, state_ssm_im, meta_tokens,
              norm1, w_in, conv_w, lam_re, lam_im, log_dt, ssm_b_re, ssm_b_im, ssm_c_re, ssm_c_im,
              ssm_d, w_glu, w_conv_out, w_ssm_out, w_o, norm2, w_coarse, w_fine, w_gate, w_up,
              w_down, final_norm):
    stacked = (norm1, w_in, conv_w, lam_re, lam_im, log_dt, ssm_b_re, ssm_b_im, ssm_c_re, ssm_c_im,
               ssm_d, w_glu, w_conv_out, w_ssm_out, w_o, norm2, w_coarse, w_fine, w_gate, w_up, w_down)
    bp = x_prompt.shape[0]
    meta = jnp.broadcast_to(meta_tokens.astype(x_prompt.dtype)[None], (bp, N_META, D_MODEL))
    xp = jnp.concatenate([meta, x_prompt], axis=1)
    conv0 = jnp.zeros((DEPTH, bp, CONV_W - 1, D_CONV), x_prompt.dtype)
    ssm0 = jnp.zeros((DEPTH, bp, SSM_G, SSM_P), jnp.float32)
    yp_full, new_conv_prompt, new_ssm_re_prompt, new_ssm_im_prompt = trunk(
        xp, conv0, ssm0, ssm0, stacked, final_norm)
    y_prompt = yp_full[:, N_META:]
    y_sample, new_conv_sample, new_ssm_re_sample, new_ssm_im_sample = trunk(
        x_sample, state_conv, state_ssm_re, state_ssm_im, stacked, final_norm)
    return (y_prompt, y_sample, new_conv_prompt, new_ssm_re_prompt, new_ssm_im_prompt,
            new_conv_sample, new_ssm_re_sample, new_ssm_im_sample)


_drawn_inputs = setup_inputs


def setup_inputs(seed=0):
    import zlib

    import numpy as np

    out = dict(_drawn_inputs(seed))
    spreads = {}
    factors = {}
    for name, (base, spread) in spreads.items():
        noise = np.random.default_rng([zlib.crc32(name.encode()), seed]).standard_normal(out[name].shape)
        drawn = base * np.exp(spread * noise) if base else spread * noise
        out[name] = __import__('jax').numpy.asarray(drawn.astype(out[name].dtype))
    for name, factor in factors.items():
        out[name] = (out[name] * factor).astype(out[name].dtype)
    return out
```

```python
from contextlib import ExitStack

import concourse.bass as bass
from concourse import mybir

F32 = mybir.dt.float32
F32R = mybir.dt.float32r
U32 = mybir.dt.uint32
I32 = mybir.dt.int32
ALU = mybir.AluOpType
ACT = mybir.ActivationFunctionType
AX = mybir.AxisListType

P = 128
L = 16
UW = 256
UK = 8
RAW, SPL = 2, 2
MRAW = 6
C = 68
EPS = 1e-6
TWO_PI_HI = 6.28125
TWO_PI_LO = 0.0019353071795864769
PI = 3.141592653589793
PI_SAFE = 3.1415925
FAR = 1 << 20


def build(nc, ins, outs):
    (x_prompt, x_sample, state_conv, state_re, state_im, meta, norm1, w_in, conv_w, lam_re, lam_im, log_dt,
     b_re, b_im, c_re, c_im, ssm_d, w_glu, w_co, w_so, w_o, norm2, w_coarse, w_fine, w_gate, w_up, w_down,
     final_norm) = ins
    (y_prompt, y_sample, nconv_p, nre_p, nim_p, nconv_s, nre_s, nim_s) = outs

    D = w_in.shape[1]
    DH = w_glu.shape[1]
    NB = x_sample.shape[0]
    NPC = (x_prompt.shape[1] + meta.shape[0]) // L
    NCH = NPC + NB
    T = NCH * L
    KD, KH = D // P, DH // P
    NG, NP_, NH = b_re.shape[1], b_re.shape[2], b_re.shape[3]
    NST = NG * NP_ // P
    SPF = NST // KH
    NE = w_gate.shape[1]
    NEG = w_coarse.shape[2]
    EPG = NE // NEG
    NR = NEG + NE
    DE = w_gate.shape[3]
    Q = 4
    TQ = T // Q
    JQ = L // Q
    MORE = -(-T // C)
    NITEM = MORE * NE
    PASSES = ((0, 0), (0, 1), (1, 0))

    XB, XC, XV, XS = 0, DH // UW, 2 * DH // UW, 3 * DH // UW
    GA, GB = 4 * DH // UW, (4 * DH + D) // UW

    ctx = ExitStack()
    with ctx:
        def sb(name, shape, dt=F32):
            return ctx.enter_context(nc.sbuf_tensor(name, shape, dt))

        def sem(name):
            return ctx.enter_context(nc.semaphore(name))

        def dram(name, shape, dt=F32):
            return nc.dram_tensor(name, shape, dt, kind="Internal").ap()

        vbuf = dram("vbuf", (T, D))
        ybuf = dram("ybuf", (T * 2, D))
        tab = dram("tab", (C * NITEM, 2), U32)

        ident = sb("ident", [P, P])
        vecs = sb("vecs", [P, P])
        O_N1, O_N2, O_CW = 0, KD, 2 * KD
        O_D = O_CW + 3 * KH
        O_LR = O_D + KH
        O_LI = O_LR + NST
        A1 = sb("A1", [P, 2, NST])
        A2 = sb("A2", [P, 2, NST])
        init = sb("init", [P, 2, NST, NB])
        fin = sb("fin", [P, 2, 1 + NB, NST])
        LVL = (NPC - 1).bit_length()
        coef = [sb(f"coef{x}", [P, 2, SPF]) for x in range(2)]
        cpow = sb("cpow", [P, 2 * LVL, 2, SPF])
        inic = sb("inic", [P, 2, SPF, NB])
        tA = sb("tA", [P, 2 * SPF * NCH])
        tB = sb("tB", [P, 2 * SPF * NCH])
        dcor = sb("dcor", [P, 2 * SPF * (NPC - 1)])
        dt1 = sb("dt1", [P, 2 * SPF * (NPC - 1)])
        dt2 = sb("dt2", [P, 2 * SPF * (NPC - 1)])
        stat = sb("stat", [P, 8, Q])

        base = (nc.sbuf_base + 31) // 32 * 32
        end = nc.sbuf_usable_end

        def at(name, off, shape, dt=F32):
            n = 4
            for s in shape[1:]:
                n *= s
            assert base + off + n <= end, (name, base + off + n, end)
            return nc.alloc_sbuf_tensor_at(name, shape, dt, offset=base + off)

        UNIT = UK * UW
        UB = UNIT * 4
        TB = T * 4
        a_raw, a_spl = 0, RAW * UB
        a_u = a_spl + SPL * 2 * UB
        a_m = a_u + 2 * KD * TB
        a_t = a_m + KD * TB
        a_xs = a_t + 2 * KH * TB
        a_st = a_xs + KH * TB
        a_bc = a_st + 2 * KH * TB
        a_end = a_bc + 2 * KH * P * 4 + 2 * KH * SPF * NH * 4
        raw = at("raw", a_raw, [P, RAW, UNIT])
        spH = at("spH", a_spl, [P, SPL, UNIT], F32R)
        spL = at("spL", a_spl + SPL * UB, [P, SPL, UNIT], F32R)
        uHL = at("uHL", a_u, [P, 2, KD, T], F32R)
        mrg = at("mrg", a_m, [P, KD, T])
        zp = at("zp", a_m, [P, KH, L + 2, NCH])
        zl = at("zl", a_m + (KH * (L + 2) * NCH * 4 + 63) // 64 * 64, [P, KH, 2, 1 + NB])
        tHL = at("tHL", a_t, [P, 2, KH, T], F32R)
        xs = at("xs", a_xs, [P, KH, T])
        st = at("st", a_st, [P, 2, L, 2, SPF, NCH])
        gHL = at("gHL", a_st, [P, 2, KH, T], F32R)
        BT = at("BT", a_bc, [P, KH, 2, P])
        CT = at("CT", a_bc + KH * 2 * P * 4, [P, KH, 2, SPF, NH])
        AP_ = at("AP_", a_m + (KD - 2) * TB, [P, 2 * LVL, 2, NST])
        assert 2 * LVL * 2 * NST * 4 <= 2 * TB
        xt = at("xt", a_m, [P, Q, D])
        sq = at("sq", a_st, [P, D])
        mjunk = at("mjunk", 4 * UB, [P, D])
        farc = at("farc", a_st + D * 4, [P, NITEM * 2], U32)
        a_p = (a_m + Q * D * 4 + 63) // 64 * 64
        vrow = at("vrow", a_p, [P, P])
        ldrow = at("ldrow", a_p + 512, [P, 2])
        ldx = at("ldx", a_p + 1024, [P, P])
        crow = at("crow", a_p + 1536, [P, 2, KH, P])
        srow = at("srow", a_p + 9728, [P, 2, 2, P])
        bnat = at("bnat", a_p + 11776, [P, 2, NST, NH])
        bbd = at("bbd", a_p + 15872, [P, 2, NST, 32])
        bcm = at("bcm", a_p + 24064, [P, NST, NH])
        sm = at("sm", a_p + 26112, [P, 20, NST])
        smi = at("smi", a_p + 28672, [P, NST], I32)
        assert a_p + 28800 <= a_st
        a_tmp = a_end
        tmp = at("tmp", a_tmp, [P, 2, T])
        btc = at("btc", a_tmp + 2 * TB, [P, 2, 2, P])
        ctc = at("ctc", a_tmp + 2 * TB + 2048, [P, 2, 2, SPF * 32])
        usc = at("usc", a_tmp + 2 * TB + 4096, [P, 2, T])
        a_gt = a_tmp + 4 * TB + 4096
        cvrow = at("cvrow", a_m + 9 * TB + TB // 2, [P, DH])
        assert KH * (L + 2) * NCH * 4 + 640 <= 9 * TB + TB // 2 and 9 * TB + TB // 2 + DH * 4 <= (KD - 2) * TB
        gt = at("gt", a_gt, [P, T])
        frow = at("frow", a_gt, [P, 6, P])
        xt2 = at("xt2", a_t, [P, Q, D])
        assert a_t + Q * D * 4 <= a_st + 2 * KH * TB
        a_h = (a_t + Q * D * 4 + 31) // 32 * 32
        htok = at("htok", a_h, [P, Q, D])
        a_w = a_h + Q * D * 4
        hT = at("hT", a_w, [P, 2, 2, T])
        g2b = at("g2b", a_w + 4 * TB, [P, D])
        a_k = a_w + 4 * TB + D * 4
        mraw = at("mraw", 6 * 2 * UB, [P, MRAW, UNIT])
        M_ORDER = (1, 2, 0, 3, 4, 5)
        assert 13 * UB >= a_m and 15 * UB <= a_t and 16 * UB <= a_t + 5120 and 18 * UB <= a_t + 24576
        mH = at("mH", 0, [P, 6, UNIT], F32R)
        mL = at("mL", 6 * UB, [P, 6, UNIT], F32R)
        xTH = at("xTH", a_k + 1152, [P, KD, C], F32R)
        xTL = at("xTL", a_k + 1152 + KD * C * 4, [P, KD, C], F32R)
        xg = at("xg", a_t + 24576, [P, D])
        assert 24576 + D * 4 <= Q * D * 4
        yo = at("yo", a_w + 4 * TB, [P, D])
        a_r = a_w
        sg = at("sg", a_r, [P, DE])
        act_ = at("act_", a_r + 1024, [P, DE])
        aTH = at("aTH", a_r + 2048, [P, 2, C], F32R)
        aTL = at("aTL", a_r + 2048 + 1024, [P, 2, C], F32R)
        slots = at("slots", a_k, [P, NE, 2], U32)
        idg = at("idg", a_k + 512, [P, 2], U32)
        ids = at("ids", a_k + 544, [P, 2], U32)
        wk = at("wk", a_k + 1024, [P, 2, Q])
        flag = at("flag", a_k + 1024 + 64, [P, 1], I32)
        wr = at("wr", a_k + 1152, [P, KD, NR])
        xst = at("xst", a_k + 1152 + KD * NR * 4, [P, Q, UW])
        rt = lambda name, off, shape, dt=F32: at(name, a_t + off, shape, dt)
        lg = rt("lg", 0, [P, Q, NR])
        cpad = rt("cpad", 1024, [P, Q, 8])
        m8 = rt("m8", 1280, [P, Q, 8])
        i8 = rt("i8", 1536, [P, Q, 8], U32)
        lmask = rt("lmask", 1792, [P, Q, EPG, NEG])
        lfg = rt("lfg", 2816, [P, Q, EPG])
        v8 = rt("v8", 3072, [P, Q, 8])
        j8 = rt("j8", 3328, [P, Q, 8], U32)
        oh4 = rt("oh4", 3584, [P, Q, NEG])
        rs = rt("rs", 4096, [P, 24, Q])
        ek = rt("ek", 5120, [P, 2, Q, NE])
        esum = rt("esum", 6400, [P, Q, NE])
        ep = rt("ep", 7168, [P, 2, Q, NE])
        trow = rt("trow", 8320, [P, Q, 2], U32)
        tval = rt("tval", 8448, [P, Q, 2, 2], U32)
        cex = rt("cex", 8704, [P, Q, NEG])
        lst = rt("lst", 9216, [P, P])
        one = rt("one", 9728, [P, P])
        iota_e = rt("iota_e", 10240, [P, NE])
        toki = rt("toki", 10368, [P, Q])
        cnt = rt("cnt", 10496, [P, NE])
        vst = at("vst", a_t + 13312, [P, 2, D // 2])
        ogu = at("ogu", 0, [P, 2, KD, DE])
        odn = at("odn", 2 * KD * DE * 4, [P, 2, D])
        oxT = at("oxT", a_m, [P, KD, C])
        oaT = at("oaT", a_m + KD * C * 4, [P, 2, C])
        oslots = at("oslots", a_m + KD * C * 4 + 2 * C * 4 + 64, [P, NITEM, 2], U32)
        yk = at("yk", 0, [P, 2, 2, D])
        fnb = at("fnb", 4 * D * 4, [P, D])
        fsq = at("fsq", 5 * D * 4, [P, 2, D])

        PS = ctx.enter_context(nc.psum_tensor("PS", [P, 8, 512], F32))
        B_BU, B_Y, B_TR = 4, 6, 7

        raw_in = [sem(f"raw_in{s}") for s in range(RAW)]
        hi_done, lo_done, unit_used = sem("hi_done"), sem("lo_done"), sem("unit_used")
        grp_done = sem("grp_done")
        dve_read = sem("dve_read")
        sig_done = sem("sig_done")
        idt = sem("idt")
        x_in = [sem(f"x_in{q}") for q in range(Q)]
        prm_in, b_in, c_in, cv_in, wr_in = sem("prm_in"), sem("b_in"), sem("c_in"), sem("cv_in"), sem("wr_in")
        pl = sem("pl")
        idn = sem("idn")
        far_in = sem("far_in")
        tab_ok = sem("tab_ok")
        d_s5 = sem("d_s5")
        d_cc = sem("d_cc")
        d_in = sem("d_in")
        a_in_ = sem("a_in_")
        ss_done, rs_done, xn_done = sem("ss_done"), sem("rs_done"), sem("xn_done")
        xtr = sem("xtr")
        uh_done, ul_done = sem("uh_done"), sem("ul_done")
        ptr = sem("ptr")
        ptr_read = sem("ptr_read")
        a_mth = sem("a_mth")
        d_mth = sem("d_mth")
        s5_par = sem("s5_par")
        z_done = sem("z_done")
        t_done, th_done, tl_done = sem("t_done"), sem("th_done"), sem("tl_done")
        xs_done = sem("xs_done")
        cpy_done = sem("cpy_done")
        bu_done, bu_read = sem("bu_done"), sem("bu_read")
        cf_done = sem("cf_done")
        loc = sem("loc")
        loc_done = sem("loc_done")
        cor_done = sem("cor_done")
        y_done, y_read = sem("y_done"), sem("y_read")
        ysq, ysg = sem("ysq"), sem("ysg")
        ys1 = sem("ys1")
        yw = sem("yw")
        gel_done = sem("gel_done")
        yh_done, yl_done = sem("yh_done"), sem("yl_done")
        gp_done, gh_done, gl_done = sem("gp_done"), sem("gh_done"), sem("gl_done")
        mh_done, ml_done = sem("mh_done"), sem("ml_done")
        nst = sem("nst")
        nst_read = sem("nst_read")
        out_in = sem("out_in")
        xt2_in = sem("xt2_in")
        hT_done, htr, htk_done = sem("hT_done"), sem("htr"), sem("htk_done")
        hrow = [sem("hrow0"), sem("hrow1")]
        res_done, xst_done, wr_done, mg_done = sem("res_done"), sem("xst_done"), sem("wr_done"), sem("mg_done")
        ldx_done, bb_done, ctz, zl_done, f_sq = (sem("ldx_done"), sem("bb_done"), sem("ctz"), sem("zl_done"),
                                                 sem("f_sq"))
        pst = sem("pst")
        xgz = sem("xgz")
        lg_done = sem("lg_done")
        g2_in = sem("g2_in")
        h_ss, h_rs = sem("h_ss"), sem("h_rs")
        v_done, v_out = sem("v_done"), [sem("v_out0"), sem("v_out1")]
        r_exp, r_arg = sem("r_exp"), sem("r_arg")
        rdc = sem("rdc")
        cst = sem("cst")
        es_done, pos_done = sem("es_done"), sem("pos_done")
        rt_done = sem("rt_done")
        sc_out = [sem(f"sc_out{n}") for n in range(8)]
        sl_in = sem("sl_in")
        m_in = [sem(f"m_in{s}") for s in range(MRAW)]
        mhi, mlo = sem("mhi"), sem("mlo")
        gu_half, gu_full, dn_done = sem("gu_half"), sem("gu_full"), sem("dn_done")
        ix_done = sem("ix_done")
        xg_in = sem("xg_in")
        xg_tr = sem("xg_tr")
        xh_done, xl_done = sem("xh_done"), sem("xl_done")
        silu_done, am_done, a_tr, ah_done, al_done = (sem("silu_done"), sem("am_done"), sem("a_tr"),
                                                      sem("ah_done"), sem("al_done"))
        yo_done, yo_out = sem("yo_done"), sem("yo_out")
        o_w, o_ix, o_x, o_tr, o_tc, o_gu, o_si, o_am, o_at, o_ac, o_dn, o_ye, o_y = [
            sem("ovf_" + n) for n in "w ix x tr tc gu si am at ac dn ye y".split()]
        osl_in = sem("osl_in")
        yk_in = [sem("yk_in0"), sem("yk_in1")]
        fn_in = sem("fn_in")
        f_ss, f_add, f_rs, f_out, f_st = sem("f_ss"), sem("f_add"), sem("f_rs"), sem("f_out"), sem("f_st")
        fch = sem("fch")

        def ge(eng, s, v):
            if not (isinstance(v, int) and v <= 0):
                eng.wait_ge(s, v)

        class Own:

            def __init__(self, eng, s, start=0):
                self.eng, self.s, self.n, self.base = eng, s, 0, start

            def __call__(self, ins):
                ins.then_inc(self.s, 1)
                self.n += 1
                self.eng.wait_ge(self.s, self.base + self.n)

            def loop(self, start):
                self.base, self.n = start, 0

        n_xs = 0
        n_cv = n_xs + 2 * KH // 2
        n_xb = n_cv + 4 * KH // 2
        n_ga = n_xb + 2 * KH // 2
        n_gl = n_ga + 3 * KD // 2
        n_gb = n_gl + KH // 2
        n_wo = n_gb + 3 * KD // 2
        n_end = n_wo + 2 * KD // 2
        g_xs, g_cv, g_xb = 0, KH // 2, 3 * KH // 2
        g_ga = g_xb + KH // 2
        g_gl = g_ga + KD
        g_gb = g_gl + KH // 2
        g_wo = g_gb + KD
        NH2, ND2 = KH // 2, KD // 2
        S5_AT = dict(zip((n_cv + 8, n_cv + 14, n_xb + 2, n_xb + 7, n_ga + 5, n_ga + 11, n_ga + 17, n_ga + 23),
                         range(KH)))
        PART_AT = {u - 3 + x: (ft, x) for u, ft in S5_AT.items() for x in range(4)}

        w_in_v = w_in[0].rearrange("(k p) n -> p k n", p=P)
        w_glu_v = w_glu[0].rearrange("(k p) n -> p k n", p=P)
        w_co_v = w_co[0].rearrange("(k p) n -> p k n", p=P)
        w_so_v = w_so[0].rearrange("(k p) n -> p k n", p=P)
        w_o_v = w_o[0].rearrange("(k p) n -> p k n", p=P)
        w_gate_v = w_gate[0].rearrange("e (k p) n -> e p k n", p=P)
        w_up_v = w_up[0].rearrange("e (k p) n -> e p k n", p=P)
        w_down_v = w_down[0].rearrange("e (k p) n -> e p k n", p=P)

        def rows_of(j, prompt, sample, first):
            p0 = (j % JQ) * NCH
            got = [(p0 + 1, NPC - 1, prompt.rearrange("(c j) d -> j c d", j=L)[j]),
                   (p0 + NPC, NB, sample[:, j, :])]
            if first is not None:
                got.append((p0, 1, first[j:j + 1, :]))
            return got

        block = ctx.enter_context(nc.Block())

        def bcast(v, n):
            return v.rearrange("(a d) -> a d", a=1).to_broadcast([P, n])

        @block.sync
        def _(sp):
            def load_rows(q, dst, s):
                for j in range(q * JQ, (q + 1) * JQ):
                    for p0, n, src in rows_of(j, x_prompt[0], x_sample, meta):
                        sp.dma_start(dst[p0:p0 + n, q, :], src).then_inc(s, 16)

            for q in range(Q):
                load_rows(q, xt, x_in[q])

            slot = [0]

            def load(n, view, k0, col):
                s = slot[0] % RAW
                slot[0] += 1
                ge(sp, lo_done, n - RAW + 1)
                sp.dma_start(raw[:, s, :].rearrange("p (k c) -> p k c", k=UK),
                             view[:, k0:k0 + UK, bass.ds(col * UW, UW)]).then_inc(raw_in[s], 16)

            for g in range(NH2):
                load(n_xs + 2 * g, w_in_v, 0, g + XS)
                load(n_xs + 2 * g + 1, w_in_v, UK, g + XS)
            with sp.Fori(0, NH2) as i:
                for c, blk in enumerate((XC, XV)):
                    load(n_cv + 4 * i + 2 * c, w_in_v, 0, i + blk)
                    load(n_cv + 4 * i + 2 * c + 1, w_in_v, UK, i + blk)
            with sp.Fori(0, NH2) as i:
                load(n_xb + 2 * i, w_in_v, 0, i + XB)
                load(n_xb + 2 * i + 1, w_in_v, UK, i + XB)
            with sp.Fori(0, ND2 // 2) as i:
                for h in range(2):
                    load(n_ga + 6 * i + 3 * h, w_in_v, 0, 2 * i + h + GA)
                    load(n_ga + 6 * i + 3 * h + 1, w_in_v, UK, 2 * i + h + GA)
                    load(n_ga + 6 * i + 3 * h + 2, w_co_v, 0, 2 * i + h)
            with sp.Fori(0, NH2 // 2) as i:
                for h in range(2):
                    load(n_gl + 2 * i + h, w_glu_v, 0, 2 * i + h)
            with sp.Fori(0, ND2 // 2) as i:
                for h in range(2):
                    load(n_gb + 6 * i + 3 * h, w_in_v, 0, 2 * i + h + GB)
                    load(n_gb + 6 * i + 3 * h + 1, w_in_v, UK, 2 * i + h + GB)
                    load(n_gb + 6 * i + 3 * h + 2, w_so_v, 0, 2 * i + h)
            sp.wait_ge(gl_done, NH2)
            for q in range(Q):
                load_rows(q, xt2, xt2_in)
            with sp.Fori(0, ND2) as i:
                load(n_wo + 2 * i, w_o_v, 0, i)
                load(n_wo + 2 * i + 1, w_o_v, UK, i)

            cursor = [0]

            def mload(n, src, k):
                s = cursor[0] % MRAW
                cursor[0] += 1
                if isinstance(n, int) and n == 2:
                    sp.wait_ge(htr, ND2)
                if isinstance(n, int) and n == 3:
                    sp.wait_ge(rt_done, 1)
                if isinstance(n, int) and n == 4:
                    sp.wait_ge(sl_in, 16)
                if isinstance(n, int) and n == 5:
                    for v in v_out:
                        sp.wait_ge(v, 16 * Q)
                ge(sp, mlo, n - MRAW + 1)
                sp.dma_start(mraw[:, M_ORDER[s], :].rearrange("p (k c) -> p k c", k=k), src).then_inc(m_in[s], 16)

            def load_gu(n, e, half):
                mload(n, w_gate_v[e][:, half * UK:(half + 1) * UK, :], UK)
                mload(n + 1, w_up_v[e][:, half * UK:(half + 1) * UK, :], UK)

            def load_d(n, e):
                for h in range(2):
                    mload(n + h, w_down_v[e][:, :, h * (D // 2):(h + 1) * (D // 2)], 2)

            sp.wait_ge(ml_done, 4)
            load_gu(0, 0, 0)
            load_gu(2, 0, 1)
            load_gu(4, 1, 0)
            load_gu(6, 1, 1)

            def rest(n, e):
                load_d(n, e - 1)
                load_gu(n + 2, e + 1, 0)
                load_gu(n + 4, e + 1, 1)

            rest(8, 1)
            with sp.Fori(2, NE - 1) as e:
                rest(6 * e + 2, e)
            load_d(6 * NE - 4, NE - 2)
            load_d(6 * NE - 2, NE - 1)

            sp.wait_ge(yo_out, 16 * NE)
            sp.wait_ge(rt_done, 1)
            over = sp.value_load(flag[0:1, 0:1], min_val=0, max_val=1)
            with sp.If(over > 0):
                sp.dma_start(oslots[0:C, :, :], tab.rearrange("(s i) v -> s i v", i=NITEM)).then_inc(osl_in, 16)
                for ps in range(1, MORE):
                    with sp.Fori(0, NE) as e:
                        n = e + (ps - 1) * NE
                        sp.wait_ge(o_ye, n + 1)
                        sp.dma_start(ogu[:, 0], w_gate_v[e]).then_inc(o_w, 16)
                        sp.dma_start(ogu[:, 1], w_up_v[e]).then_inc(o_w, 16)
                        sp.dma_start(odn[:, :, :], w_down_v[e]).then_inc(o_w, 16)
                sp.wait_ge(o_y, 16 * (MORE - 1) * NE)
            sp.nop()

            sp.dma_start(fnb[:, :], bcast(final_norm, D)).then_inc(fn_in, 16)
            yv = ybuf.rearrange("(t k) d -> t k d", k=2)

            def store(q):
                sp.wait_ge(f_out, q + 1)
                for j in range(q * JQ, (q + 1) * JQ):
                    for p0, n, dst in rows_of(j, y_prompt[0], y_sample, None):
                        sp.dma_start(dst, htok[p0:p0 + n, q, :]).then_inc(f_st, 16)

            for q in range(Q):
                ge(sp, f_add, q - 1)
                sp.dma_start(yk[0:TQ, q % 2], yv[q * TQ:(q + 1) * TQ]).then_inc(yk_in[q % 2], 16)
                if q:
                    store(q - 1)
            store(Q - 1)
            sp.wait_ge(f_st, 16 * 2 * L)
            sp.wait_ge(out_in, 16 * 10)

        @block.scalar
        def _(act):
            for r0, src in ((0, norm1[0].rearrange("(k p) -> k p", p=P)),
                            (O_N2, norm2[0].rearrange("(k p) -> k p", p=P)),
                            (O_CW, conv_w[0].rearrange("w (k p) -> (w k) p", p=P)),
                            (O_D, ssm_d[0].rearrange("(k p) -> k p", p=P)),
                            (O_LR, lam_re[0].rearrange("(s g) p -> s (g p)", g=2)),
                            (O_LI, lam_im[0].rearrange("(s g) p -> s (g p)", g=2))):
                act.dma_start(vrow[r0:r0 + src.shape[0], :], src).then_inc(prm_in, 16)
            act.dma_start(ldrow[0:NST, :], log_dt[0].rearrange("(s g) -> s g", g=2)).then_inc(prm_in, 16)
            for c, src in enumerate((b_re, b_im)):
                act.dma_start(bnat[:, c], src[0].rearrange("(s g) p h -> (g p) s h", g=2)).then_inc(b_in, 16)
            for c, src in enumerate((c_re, c_im)):
                for d in range(2):
                    act.dma_start(crow[:, c, :, d * NP_:(d + 1) * NP_],
                                  src[0].rearrange("(m g) h p -> (g h) m p", g=P // NH)).then_inc(c_in, 16)
            for c, src in enumerate((state_re, state_im)):
                act.dma_start(srow[:, c], src[0].rearrange("b (s g) p -> (b s) (g p)", g=2)
                              .rearrange("(m r) x -> r m x", m=2)).then_inc(c_in, 16)

            for q in range(Q):
                act.wait_ge(x_in[q], 16 * 3 * JQ)
                if q:
                    act.wait_ge(ss_done, q)
                act.activation(sq[0:TQ, :], xt[0:TQ, q, :], ACT.Square,
                               accum_out=stat[0:TQ, 0, q:q + 1]).then_inc(ss_done, 1)
            act.wait_ge(rs_done, 1)
            act.activation(stat[0:TQ, 2, :], stat[0:TQ, 1, :], ACT.Sqrt).then_inc(a_in_, 1)
            for k in range(KD):
                if k == 0:
                    act.wait_ge(ptr_read, 1)
                act.wait_ge(xtr, k + 1)
                act.activation(uHL[:, 0, k, :], PS[:, k % 4, 0:T], ACT.Copy,
                               scale=vecs[:, k:k + 1]).then_inc(uh_done, 1)

            slot = [0]

            def hi(n):
                s = slot[0] % RAW
                slot[0] += 1
                act.wait_ge(raw_in[s], (n - s) * 8 + 16)
                ge(act, unit_used, n - SPL + 1)
                act.activation(spH[:, s, :], raw[:, s, :], ACT.Copy).then_inc(hi_done, 1)
                if isinstance(n, int) and n - 1 in S5_AT:
                    ft = S5_AT[n - 1]
                    if ft + 2 < KH:
                        bu_prepare(ft + 2, ft % 2)
                        bu_read_(ft + 2, ft % 2)
                    gelu_act(ft)

            def bu_prepare(ft, par):
                ge(act, bu_done, 8 * (ft - 1))
                act.activation(btc[:, par], BT[:, ft], ACT.Copy).then_inc(cpy_done, 1)
                act.activation(usc[:, par], xs[:, ft], ACT.Copy).then_inc(cpy_done, 1)
                ge(act, y_done, ft - 1)
                for half in range(2):
                    p0, c0 = 64 * half, NH * half
                    act.activation(ctc[p0:p0 + 64, par].rearrange("p c (s h) -> p c s h", h=32)[:, :, :, c0:c0 + NH],
                                   CT[p0:p0 + 64, ft], ACT.Copy).then_inc(cpy_done, 1)

            def bu_read_(ft, par):
                for s in range(SPF):
                    for c in range(2):
                        act.wait_ge(bu_done, ft * 8 + 2 * s + c + 1)
                        act.activation(st[:, par, :, c, s, :],
                                       PS[:, B_BU + (2 * s + c) % 3, 0:T].rearrange("p (j h) -> p j h", h=NCH),
                                       ACT.Copy).then_inc(bu_read, 1)

            def gelu_act(ft):
                act.wait_ge(y_read, ft + 1)
                ge(act, gel_done, ft)
                act.activation(gt[:, :], xs[:, ft], ACT.Square).then_inc(ysq, 1)
                act.wait_ge(yw, ft + 1)
                act.activation(gt[:, :], gt[:, :], ACT.Sigmoid, scale=1.5957691216057308).then_inc(ysg, 1)

            hi(0)
            hi(1)
            act.wait_ge(d_mth, 1)
            act.activation(sm[:, 1, :], sm[:, 0, :], ACT.Exp).then_inc(a_mth, 1)
            act.wait_ge(d_mth, 2)
            act.activation(sm[:, 4, :], sm[:, 2, :], ACT.Exp).then_inc(a_mth, 1)
            act.wait_ge(d_mth, 3)
            act.activation(sm[:, 10, :], sm[:, 7, :], ACT.Sin).then_inc(a_mth, 1)
            act.activation(sm[:, 11, :], sm[:, 9, :], ACT.Sin).then_inc(a_mth, 1)
            for g in range(NH2):
                hi(n_xs + 2 * g + 2)
                hi(n_xs + 2 * g + 3)
            act.wait_ge(dve_read, NH2)
            act.wait_ge(s5_par, 1)
            act.wait_ge(ctz, 1)
            act.wait_ge(tab_ok, 16)
            for ft in range(2):
                bu_prepare(ft, ft)
                bu_read_(ft, ft)
            act.dma_start(cvrow[0:2 * NB, :], state_conv[0].rearrange("b k d -> (b k) d")).then_inc(cv_in, 16)
            for n in range(n_cv + 2, n_xb + 2):
                hi(n)
            for g in range(NH2):
                hi(n_xb + 2 * g + 2)
                if g == 0:
                    act.wait_ge(ptr_read, 13)
                    for k in range(2):
                        r0 = k * (1 + NB)
                        act.dma_start(nconv_p[0, :, k, :], cvrow[r0:r0 + 1, :]).then_inc(out_in, 16)
                        act.dma_start(nconv_s[0, :, k, :], cvrow[r0 + 1:r0 + 1 + NB, :]).then_inc(out_in, 16)
                act.wait_ge(t_done, g + 1)
                act.activation(tHL[:, 0, 2 * g:2 * g + 2, :], tmp[:, :, :], ACT.Copy).then_inc(th_done, 1)
                hi(n_xb + 2 * g + 3)

            act.nop().then_inc(sig_done, 1)

            for g in range(ND2):
                n = n_ga + 3 * g
                hi(n + 2)
                act.wait_ge(unit_used, n + 2)
                ge(act, dve_read, g + g_ga)
                act.wait_ge(tl_done, NH2)
                act.activation(tmp[:, :, :], PS[:, 0:2, 0:T], ACT.Sigmoid).then_inc(sig_done, 1)
                hi(n + 3)
                hi(n + 4)
            act.wait_ge(y_done, KH)
            for c0, src in ((0, w_coarse), (NEG, w_fine)):
                act.dma_start(wr[:, :, c0:c0 + src.shape[2]],
                              src[0].rearrange("(k p) n -> p k n", p=P)).then_inc(wr_in, 16)
            act.wait_ge(unit_used, n_gl)
            act.wait_ge(gel_done, KH)
            for c in range(2):
                act.activation(tHL[:, 0, 4 * c:4 * c + 4, :], xs[:, 4 * c:4 * c + 4, :], ACT.Copy).then_inc(yh_done, 1)
            for g in range(NH2):
                act.wait_ge(unit_used, n_gl + g + 1)
                ge(act, gp_done, g)
                b = 2 * (g % 2)
                act.activation(tmp[:, :, :], PS[:, b:b + 2, 0:T], ACT.Sigmoid).then_inc(sig_done, 1)
                hi(n_gl + g + 2)
                act.wait_ge(gp_done, g + 1)
                act.activation(gHL[:, 0, 2 * g:2 * g + 2, :], xs[:, 2 * g:2 * g + 2, :], ACT.Copy).then_inc(gh_done, 1)
            act.wait_ge(ptr_read, 15)
            for c, (dp, ds_) in enumerate(((nre_p, nre_s), (nim_p, nim_s))):
                act.dma_start(dp[0].rearrange("b (s g) p -> (b s) (g p)", g=2), frow[0:NST, 3 * c, :]).then_inc(out_in, 16)
                rows = ds_[0].rearrange("b (s g) p -> (b s) (g p)", g=2)
                for m in range(2):
                    act.dma_start(rows[m * P:(m + 1) * P, :], frow[:, 3 * c + 1 + m, :]).then_inc(out_in, 16)
            with act.Fori(0, ND2 // 2) as i:
                for h in range(2):
                    n, g = n_gb + 6 * i + 3 * h, 2 * i + h
                    hi(n + 2)
                    act.wait_ge(unit_used, n + 2)
                    act.wait_ge(mg_done, g + 1)
                    act.activation(tmp[:, :, :], PS[:, 0:2, 0:T], ACT.Sigmoid).then_inc(sig_done, 1)
                    hi(n + 3)
                    hi(n + 4)
            act.wait_ge(mg_done, ND2 + 1)
            for c in range(4):
                act.activation(uHL[:, 0, 4 * c:4 * c + 4, :], mrg[:, 4 * c:4 * c + 4, :], ACT.Copy).then_inc(mh_done, 1)
            act.dma_start(g2b[:, :], bcast(norm2[0], D)).then_inc(g2_in, 16)
            act.wait_ge(out_in, 16 * 10)
            act.wait_ge(xt2_in, 16 * 3 * L)

            def w_o_group(i, h, tail):
                g, n = 2 * i + h, n_wo + 4 * i + 2 * h
                if not tail:
                    hi(n + 2)
                ge(act, res_done, g)
                act.activation(xst[0:TQ], xt2[0:TQ, :, bass.ds(g * UW, UW)], ACT.Copy).then_inc(xst_done, 1)
                act.wait_ge(res_done, g + 1)
                ge(act, htr, g - 1)
                act.activation(hT[:, h], PS[:, 2 * h:2 * h + 2, 0:T], ACT.Copy).then_inc(hT_done, 1)
                if not tail:
                    hi(n + 3)

            w_o_group(0, 0, False)
            w_o_group(0, 1, False)
            with act.Fori(1, ND2 // 2 - 1) as i:
                w_o_group(i, 0, False)
                w_o_group(i, 1, False)
            w_o_group(ND2 // 2 - 1, 0, False)
            w_o_group(ND2 // 2 - 1, 1, True)

            act.wait_ge(htk_done, 2 * ND2)
            for q in range(Q):
                if q:
                    act.wait_ge(h_ss, q)
                act.activation(mjunk[0:TQ, :], htok[0:TQ, q, :], ACT.Square,
                               accum_out=stat[0:TQ, 0, q:q + 1]).then_inc(h_ss, 1)
            act.wait_ge(h_rs, 1)
            act.activation(stat[0:TQ, 2, :], stat[0:TQ, 1, :], ACT.Sqrt).then_inc(a_in_, 1)
            act.wait_ge(r_arg, 1)
            act.activation(cex[0:TQ], cex[0:TQ], ACT.Exp).then_inc(r_exp, 1)
            act.wait_ge(r_arg, 2)
            act.activation(rs[0:TQ, 3, :], rs[0:TQ, 2, :], ACT.Exp).then_inc(r_exp, 1)
            for m in range(2 * Q):
                act.wait_ge(v_done, m + 1)
                q, half = m // 2, m % 2
                act.dma_start(vbuf[q * TQ:(q + 1) * TQ, half * (D // 2):(half + 1) * (D // 2)],
                              vst[0:TQ, half, :]).then_inc(v_out[half], 16)

            cursor = [0]

            def mhi_(n0, e, s, free=None):
                r = cursor[0] % MRAW
                cursor[0] += 1
                assert n0 % MRAW == r
                act.wait_ge(m_in[r], e * 16 + 16 * ((n0 - r) // MRAW + 1))
                if free is not None:
                    ge(act, *free)
                act.activation(mH[:, s, :], mraw[:, M_ORDER[r], :], ACT.Copy).then_inc(mhi, 1)

            def xh(e):
                for b in range(4):
                    act.wait_ge(xg_tr, e * 4 + b + 1)
                    act.activation(xTH[:, 4 * b:4 * b + 4, :].rearrange("p k c -> p (k c)"),
                                   PS[:, 2 + b % 2, 0:4 * C], ACT.Copy).then_inc(xh_done, 1)

            def ah(e):
                act.wait_ge(a_tr, e + 1)
                ge(act, dn_done, e)
                act.activation(aTH[:, :, :].rearrange("p k c -> p (k c)"), PS[:, 1, 0:2 * C],
                               ACT.Copy).then_inc(ah_done, 1)

            def y_out(e):
                act.wait_ge(dn_done, e + 1)
                ge(act, yo_out, e * 16)
                act.activation(yo[0:C, :].rearrange("p (n c) -> p n c", n=4), PS[0:C, 4:8, :],
                               ACT.Copy).then_inc(yo_done, 1)

            def silu(e):
                act.wait_ge(gu_full, e + 1)
                ge(act, am_done, e)
                act.activation(sg[0:C, :], PS[0:C, 0, 0:DE], ACT.Silu).then_inc(silu_done, 1)

            act.wait_ge(htr, ND2)
            for s in range(4):
                mhi_(s, 0, s)
            xh(0)

            def body(e, first, second, last):
                if not first:
                    ah(e - 1)
                    for h in range(2):
                        mhi_(2 + h, e, 4 + h, (dn_done, e - 1))
                if not (first or second):
                    y_out(e - 2)
                n0 = 4
                if not last:
                    for h in range(2):
                        mhi_(n0 + h, e, h, (gu_half, e + 1))
                silu(e)
                if not last:
                    xh(e + 1)
                    for h in range(2):
                        mhi_(n0 + 2 + h, e, 2 + h, None)

            body(0, True, False, False)
            body(1, False, True, False)
            with act.Fori(2, NE - 1) as e:
                body(e, False, False, False)
            body(NE - 1, False, False, True)
            ah(NE - 1)
            for h in range(2):
                mhi_(4 + h, NE - 1, 4 + h, (dn_done, NE - 1))
            y_out(NE - 2)
            y_out(NE - 1)

            act.wait_ge(yo_out, 16 * NE)
            over = act.value_load(flag[0:1, 0:1], min_val=0, max_val=1)
            with act.If(over > 0):
                act.nop().then_inc(o_ye, 1)
                with act.Fori(0, (MORE - 1) * NE) as n:
                    act.wait_ge(o_tr, n + 1)
                    act.activation(oxT[:, :, :].rearrange("p (b k) c -> p b (k c)", b=4), PS[:, 2:6, 0:4 * C],
                                   ACT.Copy).then_inc(o_tc, 1)
                    act.wait_ge(o_gu, n + 1)
                    act.activation(sg[0:C, :], PS[0:C, 0, 0:DE], ACT.Silu).then_inc(o_si, 1)
                    act.wait_ge(o_at, n + 1)
                    act.activation(oaT[:, :, :].rearrange("p k c -> p (k c)"), PS[:, 1, 0:2 * C],
                                   ACT.Copy).then_inc(o_ac, 1)
                    act.wait_ge(o_dn, n + 1)
                    act.activation(yo[0:C, :].rearrange("p (n c) -> p n c", n=4), PS[0:C, 4:8, :],
                                   ACT.Copy).then_inc(o_ye, 1)
            act.nop()

            for q in range(Q):
                act.wait_ge(f_add, q + 1)
                if q:
                    act.wait_ge(f_ss, q)
                act.activation(fsq[0:TQ, q % 2, :], htok[0:TQ, q, :], ACT.Square,
                               accum_out=stat[0:TQ, 4, q:q + 1]).then_inc(f_ss, 1)
                act.wait_ge(f_rs, q + 1)
                act.activation(stat[0:TQ, 6, q:q + 1], stat[0:TQ, 5, q:q + 1], ACT.Sqrt).then_inc(f_sq, 1)

        @block.tensor
        def _(pe):
            PT = (spH, spL)
            batch = [0]

            def transposes(pairs, wait_batch=True):
                k = batch[0]
                batch[0] += 1
                if wait_batch:
                    ge(pe, ptr_read, k - 1)
                b = 6 + k % 2
                for c0, src in pairs:
                    rows, cols = src.shape[0], src.shape[1]
                    ins = pe.transpose(PS[0:cols, b, c0:c0 + rows], src, ident[0:rows, 0:rows])
                ins.then_inc(ptr, 1)

            pe.wait_ge(idn, 2)
            pe.wait_ge(prm_in, 16 * 7)
            pe.wait_ge(ldx_done, 1)
            transposes([(0, vrow[:, :]), (P, ldx[0:NST, :])])
            for k in range(KD):
                if k == 0:
                    pe.wait_ge(xn_done, Q)
                ge(pe, ul_done, k - 3)
                for q in range(Q):
                    ins = pe.transpose(PS[:, k % 4, q * TQ:(q + 1) * TQ], xt[0:TQ, q, k * P:(k + 1) * P],
                                       ident[0:TQ, 0:TQ])
                ins.then_inc(xtr, 1)
            pe.wait_ge(ul_done, KD)

            slot = [0]

            def products(n, b, rhs, k0, first, last):
                s = slot[0] % SPL
                slot[0] += 1
                if isinstance(n, int) and n in S5_AT:
                    ft = S5_AT[n]
                    if ft in (2, 3):
                        pe.wait_ge(ptr_read, batch[0])
                    y_s5(ft, ft % 2)
                    if ft + 2 < KH:
                        bu(ft + 2, ft % 2)
                pe.wait_ge(lo_done, n + 1)
                for m in range(2):
                    for k in range(UK):
                        for w, a in PASSES:
                            ins = pe.matmul(PS[:, b + m, 0:T], PT[w][:, s, k * UW + m * P:k * UW + (m + 1) * P],
                                            rhs[:, a, k0 + k, :], start=first and k == 0 and (w, a) == (0, 0),
                                            stop=last and k == UK - 1 and (w, a) == PASSES[-1])
                ins.then_inc(unit_used, 1)

            def group(n, b, rhs, units=2):
                for u in range(units):
                    products(n + u, b, rhs, u * UK, u == 0, u == units - 1)

            def bu(ft, par):
                pe.wait_ge(cpy_done, ft * 4 + 2)
                for s in range(SPF):
                    for c in range(2):
                        m = 2 * s + c
                        if m >= 3:
                            pe.wait_ge(bu_read, ft * 8 + m - 2)
                        elif m == 0:
                            ge(pe, bu_read, ft * 8)
                        pe.matmul(PS[:, B_BU + m % 3, 0:T], btc[32 * s:32 * s + 32, par, c, :],
                                  usc[32 * s:32 * s + 32, par, :], start=True, stop=True).then_inc(bu_done, 1)

            def y_s5(ft, par):
                pe.wait_ge(cor_done, ft + 1)
                pe.wait_ge(cpy_done, ft * 4 + 4)
                ge(pe, y_read, ft)
                for s in range(SPF):
                    for c in range(2):
                        ins = pe.matmul(PS[32 * s:32 * s + 32, 7, 0:T], ctc[:, par, c, 32 * s:32 * s + 32],
                                        st[:, par, :, c, s, :], start=c == 0, stop=c == 1,
                                        tile_position=(0, 32 * s))
                ins.then_inc(y_done, 1)

            group(n_xs, 0, uHL)
            pe.wait_ge(bb_done, 1)
            for c in range(2):
                for b in range(2):
                    transposes([(P * f, bbd[:, c, SPF * (4 * b + f):SPF * (4 * b + f + 1), :]
                                 .rearrange("p s x -> p (s x)")) for f in range(4)])
            pe.wait_ge(c_in, 16 * 6)
            for c in range(2):
                for b in range(2):
                    transposes([(P * f, crow[:, c, 4 * b + f, :]) for f in range(4)])
            transposes([(P * (2 * c + m), srow[:, c, m, :]) for c in range(2) for m in range(2)])
            for g in range(1, NH2):
                ge(pe, dve_read, g - 1)
                group(n_xs + 2 * g, 2 * (g % 2), uHL)
            pe.wait_ge(ptr_read, batch[0])
            pe.wait_ge(ctz, 1)
            for ft in range(2):
                bu(ft, ft)
            for i in range(NH2):
                for c in range(2):
                    pe.wait_ge(dve_read, 2 * i + g_cv + c - 1)
                    group(n_cv + 4 * i + 2 * c, 2 * c, uHL)
            pe.wait_ge(cv_in, 16)
            pe.wait_ge(bu_read, 32)
            pe.wait_ge(y_read, 2)
            transposes([(2 * NB * f, cvrow[0:2 * NB, P * f:P * (f + 1)]) for f in range(KH)])
            pe.wait_ge(zl_done, 1)
            for b in range(2):
                transposes([(P * f, zl[:, 4 * b + f].rearrange("p k b -> p (k b)")) for f in range(4)])
            for g in range(NH2):
                ge(pe, dve_read, g_xb + g - 1)
                group(n_xb + 2 * g, 2 * (g % 2), uHL)

            for g in range(ND2):
                n = n_ga + 3 * g
                pe.wait_ge(dve_read, g + g_ga - 1)
                if g:
                    pe.wait_ge(sig_done, g + 1)
                group(n, 0, uHL)
                pe.wait_ge(dve_read, g + g_ga)
                ge(pe, tl_done, NH2)
                group(n + 2, 2, tHL, 1)
            pe.wait_ge(y_read, KH)
            rows = [src for c in range(2) for src in
                    (fin[:, c, 0, :], fin[:, c, 1:5, :].rearrange("p b s -> p (b s)"),
                     fin[:, c, 5:9, :].rearrange("p b s -> p (b s)"))]
            transposes([(P * x, src) for x, src in enumerate(rows[:4])])
            transposes([(P * x, src) for x, src in enumerate(rows[4:])])
            for g in range(NH2):
                if g == 0:
                    pe.wait_ge(yl_done, 2)
                    pe.wait_ge(sig_done, ND2 + 1)
                elif g == 1:
                    pe.wait_ge(dve_read, g_ga + ND2)
                else:
                    pe.wait_ge(sig_done, ND2 + g)
                group(n_gl + g, 2 * (g % 2), tHL, 1)
            pe.wait_ge(ptr_read, batch[0])
            pe.wait_ge(gl_done, NH2)
            with pe.Fori(0, ND2 // 2) as i:
                for h in range(2):
                    n, g = n_gb + 6 * i + 3 * h, 2 * i + h
                    pe.wait_ge(sig_done, g + ND2 + NH2 + 1)
                    group(n, 0, uHL)
                    pe.wait_ge(dve_read, g + g_ga + ND2)
                    group(n + 2, 2, gHL, 1)

            def after(g, h, first, last=False):
                pe.wait_ge(hT_done, g + 1)
                for m in range(2):
                    ge(pe, htk_done, 2 * g + m - 1)
                    for q in range(Q):
                        ins = pe.transpose(PS[0:TQ, 4 + m, q * P:(q + 1) * P], hT[:, h, m, q * TQ:(q + 1) * TQ],
                                           ident[:, :])
                    ins.then_inc(hrow[m], 1)
                for m in range(2):
                    for q in range(Q):
                        ins = pe.matmul(PS[0:TQ, 6, q * NR:(q + 1) * NR], hT[:, h, m, q * TQ:(q + 1) * TQ],
                                        wr[:, 2 * g + m, :], start=first and m == 0 and q == 0, stop=last and m == 1,
                                        skip_group_check=True)
                ins.then_inc(htr, 1)

            def w_o_group(i, h, first):
                g, n = 2 * i + h, n_wo + 4 * i + 2 * h
                if isinstance(g, int) and g == 0:
                    pe.wait_ge(sig_done, 2 * ND2 + NH2 + 1)
                    pe.wait_ge(ml_done, 2)
                elif isinstance(g, int) and g == 1:
                    pe.wait_ge(dve_read, g_ga + 2 * ND2)
                else:
                    pe.wait_ge(hT_done, g - 1)
                products(n, 2 * h, uHL, 0, True, False)
                if isinstance(g, int) and g == 0:
                    pe.wait_ge(ml_done, 4)
                    pe.wait_ge(wr_done, 1)
                else:
                    after(g - 1, 1 - h, isinstance(g, int) and g == 1)
                products(n + 1, 2 * h, uHL, UK, False, True)
                pe.wait_ge(xst_done, g + 1)
                for m in range(2):
                    for q in range(Q):
                        ins = pe.matmul(PS[:, 2 * h + m, q * TQ:(q + 1) * TQ], xst[0:TQ, q, m * P:(m + 1) * P],
                                        ident[0:TQ, 0:TQ], start=False, stop=True, skip_group_check=True)
                ins.then_inc(res_done, 1)

            w_o_group(0, 0, True)
            w_o_group(0, 1, False)
            with pe.Fori(1, ND2 // 2) as i:
                w_o_group(i, 0, False)
                w_o_group(i, 1, False)
            after(ND2 - 1, 1, False, True)

            pe.wait_ge(cst, 6)
            pe.wait_ge(es_done, 1)
            for q in range(Q):
                for r in range(q + 1):
                    pe.matmul(PS[0:TQ, 7, q * NE:(q + 1) * NE], lst[0:TQ, 0:TQ] if r == q else one[0:TQ, 0:TQ],
                              esum[0:TQ, r, :], start=r == 0, stop=r == q)
            for r in range(Q):
                ins = pe.matmul(PS[0:TQ, 7, Q * NE:(Q + 1) * NE], one[0:TQ, 0:TQ], esum[0:TQ, r, :],
                                start=r == 0, stop=r == Q - 1)
            ins.then_inc(pos_done, 1)

            MT = (mH, mL)
            XT, AT = (xTH, xTL), (aTH, aTL)

            def xt_(e):
                pe.wait_ge(xg_in, e * 16 + 16)
                for b in range(4):
                    ge(pe, xl_done, 4 * e + b - 1)
                    for k in range(4):
                        ins = pe.transpose(PS[:, 2 + b % 2, k * C:(k + 1) * C],
                                           xg[0:C, (4 * b + k) * P:(4 * b + k + 1) * P], ident[0:C, 0:C])
                    ins.then_inc(xg_tr, 1)

            def gate_up(e, n0):
                pe.wait_ge(xl_done, e * 4 + 4)
                ge(pe, am_done, e)
                for half in range(2):
                    pe.wait_ge(mlo, n0 + 2 * half + 2)
                    for k in range(UK):
                        for w, a in PASSES:
                            ins = pe.matmul(PS[0:C, 0, 0:2 * DE], XT[a][:, half * UK + k, :],
                                            MT[w][:, 2 * half:2 * half + 2, k * DE:(k + 1) * DE],
                                            start=half == 0 and k == 0 and (w, a) == (0, 0),
                                            stop=half == 1 and k == UK - 1 and (w, a) == PASSES[-1])
                    ins.then_inc(gu_full if half else gu_half, 1)

            def at_(e):
                pe.wait_ge(am_done, e + 1)
                ge(pe, al_done, e)
                for k in range(2):
                    ins = pe.transpose(PS[:, 1, k * C:(k + 1) * C], act_[0:C, k * P:(k + 1) * P], ident[0:C, 0:C])
                ins.then_inc(a_tr, 1)

            def down(e, n0):
                pe.wait_ge(al_done, e + 1)
                ge(pe, yo_done, e)
                pe.wait_ge(mlo, n0 + 2)
                for c in range(4):
                    for k in range(2):
                        for w, a in PASSES:
                            o = k * (D // 2) + (c % 2) * 512
                            ins = pe.matmul(PS[0:C, 4 + c, :], AT[a][:, k, :], MT[w][:, 4 + c // 2, o:o + 512],
                                            start=k == 0 and (w, a) == (0, 0), stop=k == 1 and (w, a) == PASSES[-1])
                ins.then_inc(dn_done, 1)

            def body(e, n0, first, last):
                if not first:
                    at_(e - 1)
                gate_up(e, n0)
                if not last:
                    xt_(e + 1)
                if not first:
                    down(e - 1, 6 * e + 2)

            xt_(0)
            body(0, 0, True, False)
            body(1, 4, False, False)
            with pe.Fori(2, NE - 1) as e:
                body(e, 6 * e - 2, False, False)
            body(NE - 1, 6 * (NE - 1) - 2, False, True)
            at_(NE - 1)
            down(NE - 1, 6 * NE - 2)

            pe.wait_ge(yo_out, 16 * NE)
            over = pe.value_load(flag[0:1, 0:1], min_val=0, max_val=1)
            with pe.If(over > 0):
                with pe.Fori(0, (MORE - 1) * NE) as n:
                    pe.wait_ge(o_x, n * 16 + 16)
                    for k in range(KD):
                        ins = pe.transpose(PS[:, 2 + k // 4, (k % 4) * C:(k % 4 + 1) * C],
                                           xg[0:C, k * P:(k + 1) * P], ident[0:C, 0:C])
                    ins.then_inc(o_tr, 1)
                    pe.wait_ge(o_tc, n + 1)
                    pe.wait_ge(o_w, n * 48 + 48)
                    for k in range(KD):
                        ins = pe.matmul(PS[0:C, 0, 0:2 * DE], oxT[:, k, :], ogu[:, :, k, :],
                                        start=k == 0, stop=k == KD - 1)
                    ins.then_inc(o_gu, 1)
                    pe.wait_ge(o_am, n + 1)
                    for k in range(2):
                        ins = pe.transpose(PS[:, 1, k * C:(k + 1) * C], act_[0:C, k * P:(k + 1) * P],
                                           ident[0:C, 0:C])
                    ins.then_inc(o_at, 1)
                    pe.wait_ge(o_ac, n + 1)
                    for c in range(4):
                        for k in range(2):
                            ins = pe.matmul(PS[0:C, 4 + c, :], oaT[:, k, :], odn[:, k, c * 512:(c + 1) * 512],
                                            start=k == 0, stop=k == 1)
                    ins.then_inc(o_dn, 1)
            pe.nop()

        @block.vector
        def _(dve):
            slot = [0]

            def lo(n):
                s = slot[0] % RAW
                slot[0] += 1
                dve.wait_ge(hi_done, n + 1)
                dve.tensor_tensor(spL[:, s, :], raw[:, s, :], spH[:, s, :].bitcast(F32),
                                  ALU.subtract).then_inc(lo_done, 1)
                if isinstance(n, int) and n in PART_AT:
                    correct(*PART_AT[n])
                if isinstance(n, int) and n - 1 in S5_AT:
                    y_gelu(S5_AT[n - 1])

            TT, TS = dve.tensor_tensor, dve.tensor_scalar

            def correct(ft, x):
                par = ft % 2
                cc = Own(dve, d_cc, ft * 4 * (L - 1) + 16 * x)
                shape = [P, 2, SPF, NPC - 1]
                a1 = A1[:, :, ft * SPF:(ft + 1) * SPF].unsqueeze(3).to_broadcast(shape)
                a2 = A2[:, :, ft * SPF:(ft + 1) * SPF].unsqueeze(3).to_broadcast(shape)
                view = lambda t: t.rearrange("p (c s h) -> p c s h", c=2, s=SPF)
                w1, w2, dd = view(dt1[:, :]), view(dt2[:, :]), view(dcor[:, :])
                if x == 0:
                    dve.wait_ge(loc_done, ft + 1)
                for j in range(4 * x, min(4 * x + 4, L - 1)):
                    prev = st[:, par, L - 1, :, :, 0:NPC - 1] if j == 0 else dd
                    TT(w1, prev, a1, ALU.mult).then_inc(d_cc, 1)
                    cc.n += 1
                    cc(TT(w2, prev[:, ::-1], a2, ALU.mult))
                    cc(TT(dd, w1, w2, ALU.add))
                    TT(st[:, par, j, :, :, 1:NPC], st[:, par, j, :, :, 1:NPC], dd, ALU.add).then_inc(d_cc, 1)
                    cc.n += 1
                if x == 3:
                    dve.wait_ge(d_cc, cc.base + cc.n)
                    dve.tensor_copy(fin[:, :, :, ft * SPF:(ft + 1) * SPF],
                                    st[:, par, L - 1, :, :, NPC - 1:NCH].rearrange("p c s b -> p c b s")) \
                        .then_inc(cor_done, 1)

            def y_gelu(ft):
                dve.wait_ge(y_done, ft + 1)
                dve.scalar_tensor_tensor(out=xs[:, ft], in0=xs[:, ft], scalar=vecs[:, ft + O_D:ft + O_D + 1],
                                         in1=PS[:, 7, 0:T], op0=ALU.mult, op1=ALU.add).then_inc(y_read, 1)
                dve.wait_ge(ysq, ft + 1)
                TS(gt[:, :], gt[:, :], 0.044715, 1.0, ALU.mult, ALU.add).then_inc(ys1, 1)
                dve.wait_ge(ys1, ft + 1)
                TT(gt[:, :], gt[:, :], xs[:, ft], ALU.mult).then_inc(yw, 1)
                dve.wait_ge(ysg, ft + 1)
                TT(xs[:, ft], xs[:, ft], gt[:, :], ALU.mult).then_inc(gel_done, 1)

            own = Own(dve, d_in)
            dve.wait_ge(prm_in, 16 * 7)
            dve.tensor_copy(ldx[0:NST, :].rearrange("s (g p) -> s g p", g=2),
                            ldrow[0:NST, :].unsqueeze(2).to_broadcast([NST, 2, NP_])).then_inc(ldx_done, 1)
            dve.wait_ge(ptr, 1)
            dve.tensor_copy(vecs[:, :], PS[:, 6, 0:P]).then_inc(d_in, 1)
            own.n += 1
            dve.tensor_copy(sm[:, 0, :], PS[:, 6, P:P + NST]).then_inc(ptr_read, 1)
            dve.wait_ge(ptr_read, 1)
            dve.wait_ge(ss_done, Q)
            dve.tensor_scalar(stat[0:TQ, 1, :], stat[0:TQ, 0, :], 1.0 / D, EPS, ALU.mult, ALU.add).then_inc(rs_done, 1)
            dve.wait_ge(a_in_, 1)
            own(dve.reciprocal(stat[0:TQ, 3, :], stat[0:TQ, 2, :]))
            for q in range(Q):
                dve.tensor_scalar(xt[0:TQ, q, :], xt[0:TQ, q, :], stat[0:TQ, 3, q:q + 1], None,
                                  ALU.mult).then_inc(xn_done, 1)
            for k in range(KD):
                dve.wait_ge(uh_done, k + 1)
                dve.scalar_tensor_tensor(out=uHL[:, 1, k, :], in0=PS[:, k % 4, 0:T], scalar=vecs[:, k:k + 1],
                                         in1=uHL[:, 0, k, :].bitcast(F32), op0=ALU.mult,
                                         op1=ALU.subtract).then_inc(ul_done, 1)
            lo(0)
            lo(1)

            m = Own(dve, d_s5)
            S = lambda i: sm[:, i, :]
            lr, li = vecs[:, O_LR:O_LR + NST], vecs[:, O_LI:O_LI + NST]
            dve.nop().then_inc(d_mth, 1)
            dve.wait_ge(a_mth, 1)
            m(TT(S(3), li, S(1), ALU.mult))
            TT(S(2), lr, S(1), ALU.mult).then_inc(d_mth, 1)
            m(TS(S(5), S(3), 1.0 / (2 * PI), None, ALU.mult))
            m(dve.tensor_copy(smi[:, :], S(5)))
            m(dve.tensor_copy(S(6), smi[:, :]))
            m(dve.scalar_tensor_tensor(out=S(7), in0=S(6), scalar=-TWO_PI_HI, in1=S(3), op0=ALU.mult, op1=ALU.add))
            m(dve.scalar_tensor_tensor(out=S(7), in0=S(6), scalar=-TWO_PI_LO, in1=S(7), op0=ALU.mult, op1=ALU.add))
            m(TS(S(8), S(7), PI, -2 * PI, ALU.is_gt, ALU.mult))
            m(TT(S(7), S(7), S(8), ALU.add))
            m(TS(S(8), S(7), -PI, 2 * PI, ALU.is_lt, ALU.mult))
            m(TT(S(7), S(7), S(8), ALU.add))
            m(TS(S(9), S(7), PI / 2, None, ALU.add))
            m(TS(S(8), S(9), PI, -2 * PI, ALU.is_gt, ALU.mult))
            m(TT(S(9), S(9), S(8), ALU.add))
            m(TS(S(9), S(9), PI_SAFE, -PI_SAFE, ALU.min, ALU.max))
            TS(S(7), S(7), PI_SAFE, -PI_SAFE, ALU.min, ALU.max).then_inc(d_mth, 1)
            dve.wait_ge(a_mth, 4)
            m(TT(S(12), S(4), S(11), ALU.mult))
            m(TT(S(13), S(4), S(10), ALU.mult))
            def table(a1, a2):
                m(dve.tensor_copy(a1[:, 0, :], S(12)))
                m(dve.tensor_copy(a1[:, 1, :], S(12)))
                m(TS(a2[:, 0, :], S(13), -1.0, None, ALU.mult))
                m(dve.tensor_copy(a2[:, 1, :], S(13)))

            table(A1, A2)
            m(TS(S(14), S(12), 1.0, None, ALU.subtract))
            m(TT(S(15), lr, lr, ALU.mult))
            m(TT(S(16), li, li, ALU.mult))
            m(TT(S(15), S(15), S(16), ALU.add))
            m(dve.reciprocal(S(15), S(15)))
            m(TT(S(16), S(14), lr, ALU.mult))
            m(TT(S(17), S(13), li, ALU.mult))
            m(TT(S(16), S(16), S(17), ALU.add))
            m(TT(S(16), S(16), S(15), ALU.mult))
            m(TT(S(17), S(13), lr, ALU.mult))
            m(TT(S(18), S(14), li, ALU.mult))
            m(TT(S(17), S(17), S(18), ALU.subtract))
            m(TT(S(17), S(17), S(15), ALU.mult))
            m(dve.memset(bbd[:, :, :, :], 0.0))
            dve.wait_ge(b_in, 32)
            kk = [S(16 + c).unsqueeze(2).to_broadcast([P, NST, NH]) for c in range(2)]
            for c, op in enumerate((ALU.subtract, ALU.add)):
                m(TT(bcm[:, :, :], bnat[:, 1 - c], kk[1], ALU.mult))
                for half in range(2):
                    p = slice(64 * half, 64 * half + 64)
                    m(TT(bbd[p, c, :, NH * half:NH * (half + 1)], bnat[p, c],
                         S(16)[p].unsqueeze(2).to_broadcast([64, NST, NH]), ALU.mult))
                for half in range(2):
                    p = slice(64 * half, 64 * half + 64)
                    m(TT(bbd[p, c, :, NH * half:NH * (half + 1)], bbd[p, c, :, NH * half:NH * (half + 1)],
                         bcm[p], op))
            dve.nop().then_inc(bb_done, 1)
            for x in range(L.bit_length() - 1 + LVL):
                if x >= L.bit_length() - 1:
                    lv = x - (L.bit_length() - 1)
                    table(AP_[:, 2 * lv], AP_[:, 2 * lv + 1])
                m(TT(S(14), S(12), S(12), ALU.mult))
                m(TT(S(15), S(13), S(13), ALU.mult))
                m(TT(S(18), S(12), S(13), ALU.mult))
                m(TT(S(12), S(14), S(15), ALU.subtract))
                m(TS(S(13), S(18), 2.0, None, ALU.mult))

            def xs_read(g):
                dve.wait_ge(unit_used, n_xs + 2 * g + 2)
                b = 2 * (g % 2)
                dve.tensor_copy(xs[:, 2 * g:2 * g + 2, :], PS[:, b:b + 2, 0:T]).then_inc(dve_read, 1)

            lo(2)
            k = 1
            for c in range(2):
                for b in range(2):
                    dve.wait_ge(ptr, k + 1)
                    dve.tensor_copy(BT[:, 4 * b:4 * b + 4, c, :],
                                    PS[:, 6 + k % 2, :].rearrange("p (f x) -> p f x", f=4)).then_inc(ptr_read, 1)
                    k += 1
            for c in range(2):
                for b in range(2):
                    dve.wait_ge(ptr, k + 1)
                    for half in range(2):
                        p = slice(64 * half, 64 * half + 64)
                        src = PS[p, 6 + k % 2, :].rearrange("p (f s g h) -> p f s g h", f=4, s=SPF, g=2)[:, :, :, half, :]
                        ins = TS(CT[p, 4 * b:4 * b + 4, c], src, -1.0 if c else 1.0, None, ALU.mult)
                    ins.then_inc(ptr_read, 1)
                    k += 1
            dve.wait_ge(ptr, k + 1)
            for c in range(2):
                ins = dve.tensor_copy(init[:, c].rearrange("p s (m b) -> p m b s", m=2),
                                      PS[:, 6 + k % 2, 2 * P * c:2 * P * (c + 1)]
                                      .rearrange("p (m b s) -> p m b s", m=2, s=NST))
            ins.then_inc(ptr_read, 1)
            k += 1
            dve.wait_ge(ptr_read, k)
            dve.nop().then_inc(s5_par, 1)
            xs_read(0)
            lo(3)
            for g in range(1, NH2):
                lo(n_xs + 2 * g + 2)
                xs_read(g)
                lo(n_xs + 2 * g + 3)

            zf = zp[:, :, :, :].rearrange("p t j h -> p t (j h)")
            for i in range(NH2):
                n = n_cv + 4 * i
                lo(n + 2)
                dve.wait_ge(unit_used, n + 2)
                dve.tensor_copy(tmp[:, :, :], PS[:, 0:2, 0:T]).then_inc(dve_read, 1)
                lo(n + 3)
                lo(n + 4)
                dve.wait_ge(unit_used, n + 4)
                TT(zf[:, 2 * i:2 * i + 2, 2 * NCH:], PS[:, 2:4, 0:T], tmp[:, :, :], ALU.mult).then_inc(dve_read, 1)
                lo(n + 5)
            dve.wait_ge(dve_read, g_xb)
            own(dve.tensor_copy(zp[:, :, 0:2, 1:NPC], zp[:, :, L:L + 2, 0:NPC - 1]))
            own(dve.memset(zp[:, :, 0:2, 0:1], 0.0))
            dve.tensor_copy(zl[:, :, :, :], zp[:, :, L:L + 2, NPC - 1:NCH]).then_inc(zl_done, 1)
            dve.wait_ge(ptr, k + 1)
            own.n += 1
            dve.tensor_copy(zp[:, :, 0:2, NPC:NCH].rearrange("p t k b -> p t b k"),
                            PS[:, 6 + k % 2, 0:2 * NB * KH].rearrange("p (t b k) -> p t b k", t=KH, k=2)).then_inc(d_in, 1)
            dve.wait_ge(d_in, own.n)
            dve.nop().then_inc(ptr_read, 1)
            k += 1
            for b in range(2):
                dve.wait_ge(ptr, k + 1)
                dve.tensor_copy(cvrow[0:2 * (1 + NB), 512 * b:512 * (b + 1)],
                                PS[0:2 * (1 + NB), 6 + k % 2, :]).then_inc(ptr_read, 1)
                k += 1

            for g in range(NH2):
                n = n_xb + 2 * g
                lo(n + 2)
                if g:
                    dve.wait_ge(th_done, g)
                for m2 in range(2):
                    t = 2 * g + m2
                    wk_ = lambda kk: vecs[:, O_CW + kk * KH + t:O_CW + kk * KH + t + 1]
                    own(TS(tmp[:, m2, :], zf[:, t, 0:T], wk_(0), None, ALU.mult))
                    for kk in (1, 2):
                        own(dve.scalar_tensor_tensor(out=tmp[:, m2, :], in0=zf[:, t, kk * NCH:kk * NCH + T],
                                                     scalar=wk_(kk), in1=tmp[:, m2, :], op0=ALU.mult, op1=ALU.add))
                dve.wait_ge(unit_used, n + 2)
                b = 2 * (g % 2)
                TT(tmp[:, :, :], PS[:, b:b + 2, 0:T], tmp[:, :, :], ALU.mult).then_inc(t_done, 1)
                dve.wait_ge(t_done, g + 1)
                dve.nop().then_inc(dve_read, 1)
                lo(n + 3)
                dve.wait_ge(th_done, g + 1)
                TT(tHL[:, 1, 2 * g:2 * g + 2, :], tmp[:, :, :], tHL[:, 0, 2 * g:2 * g + 2, :].bitcast(F32),
                   ALU.subtract).then_inc(tl_done, 1)
            dve.wait_ge(out_in, 16 * 4)
            for g in range(ND2):
                n = n_ga + 3 * g
                lo(n + 2)
                lo(n + 3)
                dve.wait_ge(unit_used, n + 3)
                dve.wait_ge(sig_done, g + 2)
                TT(mrg[:, 2 * g:2 * g + 2, :], PS[:, 2:4, 0:T], tmp[:, :, :], ALU.mult).then_inc(dve_read, 1)
                lo(n + 4)
            for c in range(2):
                dve.wait_ge(yh_done, c + 1)
                TT(tHL[:, 1, 4 * c:4 * c + 4, :], xs[:, 4 * c:4 * c + 4, :], tHL[:, 0, 4 * c:4 * c + 4, :].bitcast(F32),
                   ALU.subtract).then_inc(yl_done, 1)
            for x0, x1 in ((0, 4), (4, 6)):
                dve.wait_ge(ptr, k + 1)
                for x in range(x0, x1):
                    rows = NST if x % 3 == 0 else P
                    ins = dve.tensor_copy(frow[0:rows, x, :], PS[0:rows, 6 + k % 2, P * (x - x0):P * (x - x0 + 1)])
                ins.then_inc(ptr_read, 1)
                k += 1
            for g in range(NH2):
                lo(n_gl + g + 2)
                dve.wait_ge(sig_done, ND2 + g + 2)
                TT(xs[:, 2 * g:2 * g + 2, :], xs[:, 2 * g:2 * g + 2, :], tmp[:, :, :], ALU.mult).then_inc(gp_done, 1)
                dve.wait_ge(gh_done, g + 1)
                TT(gHL[:, 1, 2 * g:2 * g + 2, :], xs[:, 2 * g:2 * g + 2, :], gHL[:, 0, 2 * g:2 * g + 2, :].bitcast(F32),
                   ALU.subtract).then_inc(gl_done, 1)
            dve.wait_ge(wr_in, 32)
            TT(wr[:, :, :], wr[:, :, :], vecs[:, O_N2:O_N2 + KD].unsqueeze(2).to_broadcast([P, KD, NR]),
               ALU.mult).then_inc(wr_done, 1)
            dve.nop().then_inc(mg_done, 1)
            with dve.Fori(0, ND2 // 2) as i:
                for h in range(2):
                    n, g = n_gb + 6 * i + 3 * h, 2 * i + h
                    lo(n + 2)
                    lo(n + 3)
                    dve.wait_ge(unit_used, n + 3)
                    dve.wait_ge(sig_done, g + ND2 + NH2 + 2)
                    TT(tmp[:, :, :], PS[:, 2:4, 0:T], tmp[:, :, :], ALU.mult).then_inc(dve_read, 1)
                    dve.wait_ge(dve_read, g + g_ga + ND2 + 1)
                    TT(mrg[:, bass.ds(2 * g, 2), :], mrg[:, bass.ds(2 * g, 2), :], tmp[:, :, :],
                       ALU.add).then_inc(mg_done, 1)
                    lo(n + 4)
            for c in range(4):
                dve.wait_ge(mh_done, c + 1)
                TT(uHL[:, 1, 4 * c:4 * c + 4, :], mrg[:, 4 * c:4 * c + 4, :], uHL[:, 0, 4 * c:4 * c + 4, :].bitcast(F32),
                   ALU.subtract).then_inc(ml_done, 1)

            def rows_out(g):
                for m2 in range(2):
                    dve.wait_ge(hrow[m2], g + 1)
                    dve.tensor_copy(htok[0:TQ, :, bass.ds((2 * g + m2) * P, P)],
                                    PS[0:TQ, 4 + m2, :].rearrange("p (q c) -> p q c", q=Q)).then_inc(htk_done, 1)

            def w_o_group(i, h, first, last):
                g, n = 2 * i + h, n_wo + 4 * i + 2 * h
                if not last:
                    lo(n + 2)
                if not first:
                    rows_out(g - 1)
                if not last:
                    lo(n + 3)

            w_o_group(0, 0, True, False)
            w_o_group(0, 1, False, False)
            with dve.Fori(1, ND2 // 2 - 1) as i:
                w_o_group(i, 0, False, False)
                w_o_group(i, 1, False, False)
            w_o_group(ND2 // 2 - 1, 0, False, False)
            w_o_group(ND2 // 2 - 1, 1, False, True)
            rows_out(ND2 - 1)

            dve.wait_ge(h_ss, Q)
            TS(stat[0:TQ, 1, :], stat[0:TQ, 0, :], 1.0 / D, EPS, ALU.mult, ALU.add).then_inc(h_rs, 1)
            dve.wait_ge(a_in_, 2)
            R = Own(dve, rdc)
            t = slice(0, TQ)
            r = lambda a, b=None: rs[t, a, :] if b is None else rs[t, a:b, :]
            bc = lambda ap, n: ap.unsqueeze(2).to_broadcast([TQ, Q, n])
            R(dve.reciprocal(stat[t, 3, :], stat[t, 2, :]))
            dve.wait_ge(htr, ND2)
            R(TT(lg[t], PS[t, 6, 0:Q * NR].rearrange("p (q n) -> p q n", q=Q), bc(stat[t, 3, :], NR), ALU.mult))
            R(dve.tensor_reduce(r(0), lg[t, :, 0:NEG], AX.X, ALU.max))
            TT(cex[t], lg[t, :, 0:NEG], bc(r(0), NEG), ALU.subtract).then_inc(r_arg, 1)
            R(dve.memset(cpad[t], -3.0e38))
            R(dve.tensor_copy(cpad[t, :, 0:NEG], lg[t, :, 0:NEG]))
            for q in range(Q):
                R(dve.max(m8[t, q], cpad[t, q]))
            for q in range(Q):
                R(dve.max_index(i8[t, q], m8[t, q], cpad[t, q]))
            R(dve.tensor_copy(r(1), i8[t, :, 0]))
            dve.wait_ge(cst, 6)
            iot = lambda n: iota_e[t, 0:n].unsqueeze(1).to_broadcast([TQ, Q, n])
            R(TT(oh4[t], iot(NEG), bc(r(1), NEG), ALU.is_equal))
            R(TT(lmask[t], lg[t, :, NEG:].rearrange("p q (g e) -> p q e g", g=NEG),
                 oh4[t].unsqueeze(2).to_broadcast([TQ, Q, EPG, NEG]), ALU.mult))
            R(dve.tensor_reduce(lfg[t], lmask[t], AX.X, ALU.add))
            for q in range(Q):
                R(dve.max(v8[t, q], lfg[t, q]))
            TT(r(2), v8[t, :, 1], v8[t, :, 0], ALU.subtract).then_inc(r_arg, 1)
            for q in range(Q):
                R(dve.max_index(j8[t, q], v8[t, q], lfg[t, q]))
            R(dve.tensor_copy(r(4), j8[t, :, 0]))
            R(dve.tensor_copy(r(5), j8[t, :, 1]))
            for kk in range(2):
                R(dve.scalar_tensor_tensor(out=r(10 + kk), in0=r(1), scalar=float(EPG), in1=r(4 + kk),
                                           op0=ALU.mult, op1=ALU.add))
                R(TT(ek[t, kk], iot(NE), bc(r(10 + kk), NE), ALU.is_equal))
            TT(esum[t], ek[t, 0], ek[t, 1], ALU.add).then_inc(es_done, 1)
            dve.wait_ge(r_exp, 2)
            R(dve.tensor_reduce(r(6), cex[t], AX.X, ALU.add))
            R(dve.reciprocal(r(7), r(6)))
            R(TS(r(8), r(3), 1.0, None, ALU.add))
            R(dve.reciprocal(r(9), r(8)))
            R(TT(wk[t, 0, :], r(9), r(7), ALU.mult))
            R(TT(wk[t, 1, :], wk[t, 0, :], r(3), ALU.mult))
            dve.wait_ge(pos_done, 1)
            pos = PS[t, 7, 0:Q * NE].rearrange("p (q e) -> p q e", q=Q)
            for kk in range(2):
                R(TT(ep[t, kk], pos, ek[t, kk], ALU.mult))
                R(dve.tensor_reduce(r(12 + kk), ep[t, kk], AX.X, ALU.add))
            R(dve.tensor_reduce(rs[t, 18, 0:1], PS[t, 7, Q * NE:(Q + 1) * NE], AX.X, ALU.max))
            R(TS(flag[t, :], rs[t, 18, 0:1], float(C), None, ALU.is_gt))
            R(dve.memset(r(14, 16), 0.0))
            for mm in range(1, MORE):
                R(dve.scalar_tensor_tensor(out=r(14, 16), in0=r(12, 14), scalar=float(C * mm), in1=r(14, 16),
                                           op0=ALU.is_ge, op1=ALU.add))
            R(dve.scalar_tensor_tensor(out=r(12, 14), in0=r(14, 16), scalar=-float(C), in1=r(12, 14),
                                       op0=ALU.mult, op1=ALU.add))
            R(dve.scalar_tensor_tensor(out=r(10, 12), in0=r(14, 16), scalar=float(NE), in1=r(10, 12),
                                       op0=ALU.mult, op1=ALU.add))
            R(dve.scalar_tensor_tensor(out=trow[t].rearrange("p q k -> p k q"), in0=r(12, 14), scalar=float(NITEM),
                                       in1=r(10, 12), op0=ALU.mult, op1=ALU.add))
            for kk in range(2):
                R(dve.tensor_copy(tval[t, :, kk, 0], toki[t, :]))
                R(TS(tval[t, :, kk, 1], toki[t, :], 2.0, float(kk), ALU.mult, ALU.add))
            dve.nop().then_inc(rt_done, 1)
            dve.wait_ge(g2_in, 16)
            for m2 in range(2 * Q):
                q, half = m2 // 2, m2 % 2
                ge(dve, v_out[half], 16 * q)
                c = slice(half * (D // 2), (half + 1) * (D // 2))
                dve.scalar_tensor_tensor(out=vst[t, half, :], in0=htok[t, q, c], scalar=stat[t, 3, q:q + 1],
                                         in1=g2b[t, c], op0=ALU.mult, op1=ALU.mult).then_inc(v_done, 1)

            cursor = [0]

            def mlo_(n0, e, s):
                rr = cursor[0] % MRAW
                cursor[0] += 1
                dve.wait_ge(mhi, e * 6 + n0 + 1)
                TT(mL[:, s, :], mraw[:, M_ORDER[rr], :], mH[:, s, :].bitcast(F32), ALU.subtract).then_inc(mlo, 1)

            def xl(e):
                for b in range(4):
                    dve.wait_ge(xh_done, e * 4 + b + 1)
                    TT(xTL[:, 4 * b:4 * b + 4, :].rearrange("p k c -> p (k c)"), PS[:, 2 + b % 2, 0:4 * C],
                       xTH[:, 4 * b:4 * b + 4, :].rearrange("p k c -> p (k c)").bitcast(F32),
                       ALU.subtract).then_inc(xl_done, 1)

            def al(e):
                dve.wait_ge(ah_done, e + 1)
                TT(aTL[:, :, :].rearrange("p k c -> p (k c)"), PS[:, 1, 0:2 * C],
                   aTH[:, :, :].rearrange("p k c -> p (k c)").bitcast(F32), ALU.subtract).then_inc(al_done, 1)

            def am(e):
                dve.wait_ge(silu_done, e + 1)
                ge(dve, a_tr, e)
                TT(act_[0:C, :], PS[0:C, 0, DE:2 * DE], sg[0:C, :], ALU.mult).then_inc(am_done, 1)

            for s in range(4):
                mlo_(s, 0, s)
            xl(0)

            def body(e, first, last):
                if not first:
                    al(e - 1)
                    for h in range(2):
                        mlo_(2 + h, e, 4 + h)
                if not last:
                    for h in range(2):
                        mlo_(4 + h, e, h)
                am(e)
                if not last:
                    xl(e + 1)
                    for h in range(2):
                        mlo_(6 + h, e, 2 + h)

            body(0, True, False)
            with dve.Fori(1, NE - 1) as e:
                body(e, False, False)
            body(NE - 1, False, True)
            al(NE - 1)
            for h in range(2):
                mlo_(4 + h, NE - 1, 4 + h)

            dve.wait_ge(yo_out, 16 * NE)
            over = dve.value_load(flag[0:1, 0:1], min_val=0, max_val=1)
            with dve.If(over > 0):
                with dve.Fori(0, (MORE - 1) * NE) as n:
                    dve.wait_ge(o_si, n + 1)
                    TT(act_[0:C, :], PS[0:C, 0, DE:2 * DE], sg[0:C, :], ALU.mult).then_inc(o_am, 1)
            dve.nop()

            fc = Own(dve, fch)
            for q in range(Q):
                dve.wait_ge(yk_in[q % 2], 16 * (q // 2 + 1))
                fc(dve.scalar_tensor_tensor(out=htok[t, q, :], in0=yk[t, q % 2, 0, :], scalar=wk[t, 0, q:q + 1],
                                            in1=htok[t, q, :], op0=ALU.mult, op1=ALU.add))
                dve.scalar_tensor_tensor(out=htok[t, q, :], in0=yk[t, q % 2, 1, :], scalar=wk[t, 1, q:q + 1],
                                         in1=htok[t, q, :], op0=ALU.mult, op1=ALU.add).then_inc(f_add, 1)
                dve.wait_ge(f_ss, q + 1)
                TS(stat[t, 5, q:q + 1], stat[t, 4, q:q + 1], 1.0 / D, EPS, ALU.mult, ALU.add).then_inc(f_rs, 1)
                dve.wait_ge(f_sq, q + 1)
                fc(dve.reciprocal(stat[t, 7, q:q + 1], stat[t, 6, q:q + 1]))
                if q == 0:
                    dve.wait_ge(fn_in, 16)
                dve.scalar_tensor_tensor(out=htok[t, q, :], in0=htok[t, q, :], scalar=stat[t, 7, q:q + 1],
                                         in1=fnb[t, :], op0=ALU.mult, op1=ALU.mult).then_inc(f_out, 1)

        @block.gpsimd
        def _(pool):
            pool.memset(ident[:, :], 0.0).then_inc(idn, 1)
            pool.wait_ge(idn, 1)
            pool.affine_select(out=ident[:, :], in_=ident[:, :], compare_op=ALU.not_equal, fill=1.0, base=0,
                               pattern=[[-1, P]], channel_multiplier=1).then_inc(idn, 1)
            pool.memset(ctc[:, :, :, :], 0.0).then_inc(ctz, 1)
            pool.memset(farc[:, :], FAR).then_inc(far_in, 1)
            pool.wait_ge(far_in, 1)
            pool.dma_start(tab.rearrange("(s i) v -> s (i v)", i=NITEM), farc[0:C, :]).then_inc(tab_ok, 16)

            TT = pool.tensor_tensor

            def steps(k, t1, t2, prev, a1, a2, cur):
                TT(t1, prev, a1, ALU.mult).then_inc(loc, 1)
                k.n += 1
                k(TT(t2, prev[:, ::-1], a2, ALU.mult))
                k(TT(cur, cur, t1, ALU.add))
                k(TT(cur, cur, t2, ALU.add))

            pool.wait_ge(s5_par, 1)
            with pool.Fori(0, KH // 2) as i:
                for par in range(2):
                    ft = 2 * i + par
                    f = bass.ds(ft * SPF, SPF)
                    for dst, src in zip(coef, (A1, A2)):
                        pool.tensor_copy(dst[:, :, :], src[:, :, f]).then_inc(cf_done, 1)
                    pool.tensor_copy(cpow[:, :, :, :], AP_[:, :, :, f]).then_inc(cf_done, 1)
                    pool.tensor_copy(inic[:, :, :, :], init[:, :, f, :]).then_inc(cf_done, 1)
                    fA1, fA2 = coef
                    k = Own(pool, loc, ft * (4 * (L + LVL)))
                    pool.wait_ge(cf_done, ft * 4 + 4)
                    pool.wait_ge(bu_read, ft * 8 + 8)
                    for j in range(L):
                        c0 = NPC if j == 0 else 0
                        n = NCH - c0
                        prev = inic[:, :, :, :] if j == 0 else st[:, par, j - 1, :, :, :]
                        t1, t2 = [x[:, 0:2 * SPF * n].rearrange("p (c s h) -> p c s h", c=2, s=SPF) for x in (tA, tB)]
                        a1, a2 = [x[:, :, :].unsqueeze(3).to_broadcast([P, 2, SPF, n]) for x in (fA1, fA2)]
                        steps(k, t1, t2, prev, a1, a2, st[:, par, j, :, :, c0:])
                    for lv in range(LVL):
                        n = NPC - (1 << lv)
                        t1, t2 = [x[:, 0:2 * SPF * n].rearrange("p (c s h) -> p c s h", c=2, s=SPF) for x in (tA, tB)]
                        a1, a2 = [cpow[:, 2 * lv + x, :, :].unsqueeze(3).to_broadcast([P, 2, SPF, n]) for x in (0, 1)]
                        steps(k, t1, t2, st[:, par, L - 1, :, :, 0:n], a1, a2, st[:, par, L - 1, :, :, 1 << lv:NPC])
                    pool.nop().then_inc(loc_done, 1)

            pool.wait_ge(res_done, ND2)
            pool.memset(one[:, :], 1.0).then_inc(cst, 1)
            pool.iota(iota_e[:, :], pattern=[[1, NE]], base=0, channel_multiplier=0,
                      allow_small_or_imprecise_dtypes=True).then_inc(cst, 1)
            pool.iota(toki[:, :], pattern=[[TQ, Q]], base=0, channel_multiplier=1,
                      allow_small_or_imprecise_dtypes=True).then_inc(cst, 1)
            pool.wait_ge(cst, 3)
            pool.affine_select(out=lst[:, :], in_=one[:, :], compare_op=ALU.is_gt, fill=0.0, base=0,
                               pattern=[[1, P]], channel_multiplier=-1).then_inc(cst, 1)
            pool.memset(xg[:, :], 0.0).then_inc(cst, 1)
            pool.memset(cnt[:, :], 0.0).then_inc(cst, 1)

            pool.wait_ge(tab_ok, 16)
            pool.wait_ge(rt_done, 1)
            for q in range(Q):
                for kk in range(2):
                    pool.indirect_dma_start(
                        out=tab[:, :], out_offset=bass.IndirectOffsetOnAxis(ap=trow[0:TQ, q, kk:kk + 1], axis=0),
                        in_=tval[0:TQ, q, kk, :], in_offset=None, bounds_check=C * NITEM - 1,
                        oob_is_err=False).then_inc(sc_out[2 * q + kk], 16)
            for x in range(8):
                pool.wait_ge(sc_out[x], 16)
            pool.dma_start(slots[0:C, :, :], tab.rearrange("(s i) v -> s i v", i=NITEM)[:, 0:NE, :]).then_inc(sl_in, 16)
            pool.wait_ge(sl_in, 16)
            for half in range(2):
                pool.wait_ge(v_out[half], 16 * Q)

            def gather(s):
                pool.nop().then_inc(pl, 1)
                pool.indirect_dma_start(out=xg[0:C, :], out_offset=None, in_=vbuf[:, :],
                                        in_offset=bass.IndirectOffsetOnAxis(ap=idg[0:C, 0:1], axis=0),
                                        bounds_check=T - 1, oob_is_err=False).then_inc(s, 16)

            def scatter(s):
                pool.nop().then_inc(pl, 1)
                pool.indirect_dma_start(out=ybuf[:, :],
                                        out_offset=bass.IndirectOffsetOnAxis(ap=ids[0:C, 1:2], axis=0),
                                        in_=yo[0:C, :], in_offset=None, bounds_check=2 * T - 1,
                                        oob_is_err=False).then_inc(s, 16)

            def gather_e(e):
                ge(pool, xg_in, e * 16)
                pool.tensor_copy(idg[0:C, :], slots[0:C, e, :]).then_inc(ix_done, 1)
                pool.wait_ge(ix_done, e + 1)
                ge(pool, xg_tr, e * 4)
                gather(xg_in)

            def scatter_e(e):
                ge(pool, yo_out, e * 16)
                pool.tensor_copy(ids[0:C, :], slots[0:C, e, :]).then_inc(pst, 1)
                pool.wait_ge(pst, e + 1)
                pool.wait_ge(yo_done, e + 1)
                scatter(yo_out)

            gather_e(0)
            gather_e(1)
            gather_e(2)
            with pool.Fori(2, NE - 1) as e:
                gather_e(e + 1)
                scatter_e(e - 2)
            for e in range(NE - 3, NE):
                scatter_e(e)

            pool.wait_ge(yo_out, 16 * NE)
            over = pool.value_load(flag[0:1, 0:1], min_val=0, max_val=1)
            with pool.If(over > 0):
                pool.wait_ge(osl_in, 16)
                with pool.Fori(0, (MORE - 1) * NE) as n:
                    pool.tensor_copy(idg[0:C, :], oslots[0:C, n + NE, :]).then_inc(o_ix, 1)
                    pool.tensor_copy(ids[0:C, :], oslots[0:C, n + NE, :]).then_inc(o_ix, 1)
                    pool.wait_ge(o_ix, n * 2 + 2)
                    gather(o_x)
                    pool.wait_ge(o_ye, n + 2)
                    scatter(o_y)
                    pool.wait_ge(o_y, n * 16 + 16)
            pool.nop()


_INS = ["x_prompt", "x_sample", "state_conv", "state_ssm_re", "state_ssm_im", "meta_tokens", "norm1", "w_in",
        "conv_w", "lam_re", "lam_im", "log_dt", "ssm_b_re", "ssm_b_im", "ssm_c_re", "ssm_c_im", "ssm_d", "w_glu",
        "w_conv_out", "w_ssm_out", "w_o", "norm2", "w_coarse", "w_fine", "w_gate", "w_up", "w_down", "final_norm"]


def program(nc, inputs):
    ins = [nc.dram_tensor(n, inputs[n].shape, F32, kind="ExternalInput").ap() for n in _INS]
    xp, xsm, sc, sr = (inputs[n].shape for n in ("x_prompt", "x_sample", "state_conv", "state_ssm_re"))
    shapes = [xp, xsm, (sc[0], xp[0]) + tuple(sc[2:]), (sr[0], xp[0]) + tuple(sr[2:]),
              (sr[0], xp[0]) + tuple(sr[2:]), sc, sr, sr]
    outs = [nc.dram_tensor(f"out_{i}", tuple(s), F32, kind="ExternalOutput").ap() for i, s in enumerate(shapes)]
    build(nc, ins, outs)
    return [f"out_{i}" for i in range(len(outs))]


def kernel(**inputs):
    import concourse.bacc as bacc
    import numpy as np
    from concourse.bass_utils import run_bass_kernel_spmd

    arrays = {n: np.ascontiguousarray(inputs[n]) for n in _INS}
    nc = bacc.Bacc("TRN2", target_bir_lowering=False, num_devices=1, dynamic_dma_scratch_size=2048)
    names = program(nc, arrays)
    r = run_bass_kernel_spmd(nc, [arrays], core_ids=[0])
    return tuple(r.results[0][n] for n in names)
```

```python
from contextlib import ExitStack

import concourse.bass as bass
from concourse import mybir

F32 = mybir.dt.float32
F32R = mybir.dt.float32r
BF16 = mybir.dt.bfloat16
U32 = mybir.dt.uint32
I32 = mybir.dt.int32
ALU = mybir.AluOpType
ACT = mybir.ActivationFunctionType
AX = mybir.AxisListType

P = 128
L = 16
UW = 256
UK = 8
RAW, SPL = 2, 2
MRAW = 6
C = 52
CM = 68
EPS = 1e-6
TWO_PI_HI = 6.28125
TWO_PI_LO = 0.0019353071795864769
PI = 3.141592653589793
PI_SAFE = 3.1415925
FAR = 1 << 20


def build(nc, ins, outs):
    (x_prompt, x_sample, state_conv, state_re, state_im, meta, norm1, w_in, conv_w, lam_re, lam_im, log_dt,
     b_re, b_im, c_re, c_im, ssm_d, w_glu, w_co, w_so, w_o, norm2, w_coarse, w_fine, w_gate, w_up, w_down,
     final_norm) = ins
    (y_prompt, y_sample, nconv_p, nre_p, nim_p, nconv_s, nre_s, nim_s) = outs

    D = w_in.shape[1]
    DH = w_glu.shape[1]
    NB = x_sample.shape[0]
    NPC = (x_prompt.shape[1] + meta.shape[0]) // L
    NCH = NPC + NB
    T = NCH * L
    KD, KH = D // P, DH // P
    NG, NP_, NH = b_re.shape[1], b_re.shape[2], b_re.shape[3]
    NST = NG * NP_ // P
    SPF = NST // KH
    NE = w_gate.shape[1]
    NEG = w_coarse.shape[2]
    EPG = NE // NEG
    NR = NEG + NE
    DE = w_gate.shape[3]
    Q = 4
    TQ = T // Q
    JQ = L // Q
    MORE = -(-T // C)
    NITEM = MORE * NE
    PASSES = ((0, 0), (0, 1), (1, 0))

    XB, XC, XV, XS = 0, DH // UW, 2 * DH // UW, 3 * DH // UW
    GA, GB = 4 * DH // UW, (4 * DH + D) // UW

    ctx = ExitStack()
    with ctx:
        def sb(name, shape, dt=F32):
            return ctx.enter_context(nc.sbuf_tensor(name, shape, dt))

        def sem(name):
            return ctx.enter_context(nc.semaphore(name))

        def dram(name, shape, dt=F32):
            return nc.dram_tensor(name, shape, dt, kind="Internal").ap()

        vbuf = dram("vbuf", (T, D))
        ybuf = dram("ybuf", (T * 2, D))
        tab = dram("tab", (C * NITEM, 2), U32)

        ident = sb("ident", [P, P])
        vecs = sb("vecs", [P, P])
        O_N2, O_CW = KD, 2 * KD
        O_D = O_CW + 3 * KH
        O_LR = O_D + KH
        O_LI = O_LR + NST
        A1 = sb("A1", [P, 2, NST])
        A2 = sb("A2", [P, 2, NST])
        init = sb("init", [P, 2, NST, NB])
        fin = sb("fin", [P, 2, 1 + NB, NST])
        LVL = (NPC - 1).bit_length()
        coef = [sb(f"coef{x}", [P, 2, SPF]) for x in range(2)]
        cpow = sb("cpow", [P, 2 * LVL, 2, SPF])
        inic = sb("inic", [P, 2, SPF, NB])
        n_loc, n_cor = 2 * SPF * NCH, 2 * SPF * (NPC - 1)
        work = sb("work", [P, 2 * n_loc + 3 * n_cor])
        tA, tB = work[:, 0:n_loc], work[:, n_loc:2 * n_loc]
        dcor, dt1, dt2 = [work[:, 2 * n_loc + x * n_cor:2 * n_loc + (x + 1) * n_cor] for x in range(3)]
        stat = sb("stat", [P, 9, Q])

        base = (nc.sbuf_base + 31) // 32 * 32
        end = nc.sbuf_usable_end

        def at(name, off, shape, dt=F32):
            n = 4
            for s in shape[1:]:
                n *= s
            assert base + off + n <= end, (name, base + off + n, end)
            return nc.alloc_sbuf_tensor_at(name, shape, dt, offset=base + off)

        UNIT = UK * UW
        UB = UNIT * 4
        TB = T * 4
        a_raw, a_spl = 0, RAW * UB
        a_u = a_spl + SPL * 2 * UB
        a_m = a_u + 2 * KD * TB
        a_t = a_m + KD * TB
        a_xs = a_t + 2 * KH * TB
        a_st = a_xs + KH * TB
        a_bc = a_st + 2 * KH * TB
        a_end = a_bc + 2 * KH * P * 4 + 2 * KH * SPF * NH * 4
        raw = at("raw", a_raw, [P, RAW, UNIT])
        spH = at("spH", a_spl, [P, SPL, UNIT], F32R)
        spL = at("spL", a_spl + SPL * UB, [P, SPL, UNIT], F32R)
        uHL = at("uHL", a_u, [P, 2, KD, T], F32R)
        mrg = at("mrg", a_m, [P, KD, T])
        zp = at("zp", a_m, [P, KH, L + 2, NCH])
        zl = at("zl", a_m + (KH * (L + 2) * NCH * 4 + 63) // 64 * 64, [P, KH, 2, 1 + NB])
        tHL = at("tHL", a_t, [P, 2, KH, T], F32R)
        xs = at("xs", a_xs, [P, KH, T])
        st = at("st", a_st, [P, 2, L, 2, SPF, NCH])
        gHL = at("gHL", a_st, [P, 2, KH, T], F32R)
        BT = at("BT", a_bc, [P, KH, 2, P])
        CT = at("CT", a_bc + KH * 2 * P * 4, [P, KH, 2, SPF, NH])
        AP_ = at("AP_", a_m + (KD - 2) * TB, [P, 2 * LVL, 2, NST])
        assert 2 * LVL * 2 * NST * 4 <= 2 * TB
        xt = at("xt", a_m, [P, Q, D])
        sq = at("sq", a_st, [P, D])
        farc = at("farc", a_st + D * 4, [P, NITEM * 2], U32)
        a_p = (a_m + Q * D * 4 + 63) // 64 * 64
        vrow = at("vrow", a_p, [P, P])
        ldrow = at("ldrow", a_p + 512, [P, 2])
        ldx = at("ldx", a_p + 1024, [P, P])
        crow = at("crow", a_p + 1536, [P, 2, KH, P])
        srow = at("srow", a_p + 9728, [P, 2, 2, P])
        bnat = at("bnat", a_p + 11776, [P, 2, NST, NH])
        bbd = at("bbd", a_p + 15872, [P, 2, NST, 32])
        bcm = at("bcm", a_p + 24064, [P, NST, NH])
        sm = at("sm", a_p + 26112, [P, 20, NST])
        smi = at("smi", a_p + 28672, [P, NST], I32)
        assert a_p + 28800 <= a_st
        a_tmp = a_end
        tmp = at("tmp", a_tmp, [P, 2, T])
        btc = at("btc", a_tmp + 2 * TB, [P, 2, 2, P])
        ctc = at("ctc", a_tmp + 2 * TB + 2048, [P, 2, 2, SPF * 32])
        usc = at("usc", a_tmp + 2 * TB + 4096, [P, 2, T])
        a_gt = a_tmp + 4 * TB + 4096
        cvrow = at("cvrow", a_m + 9 * TB + TB // 2, [P, DH])
        assert KH * (L + 2) * NCH * 4 + 640 <= 9 * TB + TB // 2 and 9 * TB + TB // 2 + DH * 4 <= (KD - 2) * TB
        gt = at("gt", a_gt, [P, T])
        frow = at("frow", a_gt, [P, 6, P])
        a_h = a_t + Q * D * 4
        htok = at("htok", a_t, [P, Q, D])
        xt2 = at("xt2", a_h, [P, Q, D])
        assert a_h >= a_xs and a_h + Q * D * 4 <= a_bc + 2 * KH * P * 4
        a_w = a_h + Q * D * 4
        hT = at("hT", a_w, [P, 2, 2, T])
        g2b = at("g2b", a_w + 4 * TB, [P, D])
        a_k = a_w + 4 * TB + D * 4
        SQ1 = D * 3 // 4
        mjunk = work[:, 0:SQ1 // 2].bitcast(BF16)
        mraw_a = at("mraw_a", a_m, [P, MRAW // 2, UNIT])
        mraw_b = at("mraw_b", 8 * UB, [P, MRAW // 2, UNIT])
        mraw = [t[:, x, :] for t in (mraw_a, mraw_b) for x in range(MRAW // 2)]
        assert MRAW // 2 * UB <= KD * TB and 8 * UB >= a_u and 11 * UB + D * 4 <= a_m
        mHg = at("mHg", 0, [P, 4, UNIT], F32R)
        mLg = at("mLg", 4 * UB, [P, 4, UNIT], F32R)
        mHd = at("mHd", a_h, [P, 2, UNIT], F32R)
        mLd = at("mLd", a_h + 2 * UB, [P, 2, UNIT], F32R)
        mH, mL = [[g[:, x, :] for x in range(4)] + [d[:, x, :] for x in range(2)] for g, d in ((mHg, mHd), (mLg, mLd))]
        xTH = at("xTH", a_k + 1152, [P, KD, CM], F32R)
        xTL = at("xTL", a_k + 1152 + KD * CM * 4, [P, KD, CM], F32R)
        xg = at("xg", a_w + 4 * TB, [P, D])
        assert 24576 + D * 4 <= Q * D * 4
        yo = at("yo", 11 * UB, [P, D])
        a_r = a_w
        sg = at("sg", a_r, [P, DE])
        act_ = at("act_", a_r + 1024, [P, DE])
        aTH = at("aTH", a_r + 2048, [P, 2, CM], F32R)
        aTL = at("aTL", a_r + 2048 + 1024, [P, 2, CM], F32R)
        slots = at("slots", a_k, [P, NE, 2], U32)
        idg = at("idg", a_k + 512, [P, 2], U32)
        ids = at("ids", a_k + 544, [P, 2], U32)
        wk = at("wk", a_k + 1024, [P, 2, Q])
        flag = at("flag", a_k + 1024 + 64, [P, 1], I32)
        wr = at("wr", a_k + 1152, [P, KD, NR])
        xst = at("xst", a_k + 1152 + KD * NR * 4, [P, Q, UW])
        rt = lambda name, off, shape, dt=F32: at(name, 6 * UB + off, shape, dt)
        assert 6 * UB >= a_u
        lg = rt("lg", 0, [P, Q, NR])
        cpad = rt("cpad", 1024, [P, Q, 8])
        m8 = rt("m8", 1280, [P, Q, 8])
        i8 = rt("i8", 1536, [P, Q, 8], U32)
        lmask = rt("lmask", 1792, [P, Q, EPG, NEG])
        lfg = rt("lfg", 2816, [P, Q, EPG])
        v8 = rt("v8", 3072, [P, Q, 8])
        j8 = rt("j8", 3328, [P, Q, 8], U32)
        oh4 = rt("oh4", 3584, [P, Q, NEG])
        rs = rt("rs", 4096, [P, 24, Q])
        ek = rt("ek", 5120, [P, 2, Q, NE])
        esum = rt("esum", 6400, [P, Q, NE], BF16)
        ep = rt("ep", 7168, [P, 2, Q, NE])
        trow = at("trow", a_k + 576, [P, Q, 2], U32)
        tval = at("tval", a_k + 640, [P, Q, 2, 2], U32)
        cex = rt("cex", 8704, [P, Q, NEG])
        lst = rt("lst", 9216, [P, P], BF16)
        one = rt("one", 9728, [P, P], BF16)
        iota_e = rt("iota_e", 10240, [P, NE])
        toki = rt("toki", 10368, [P, Q])
        tk = rt("tk", 10432, [P, 2, 2, Q])
        iota_c = rt("iota_c", 10560, [P, C])
        oc = rt("oc", 10784, [P, 2, Q, C])
        etok = rt("etok", 12512, [P, 2, Q, NE, 2])
        efar = rt("efar", 14592, [P, NE * 2])
        assert 14592 + NE * 8 <= 2 * UB
        ogu = at("ogu", 0, [P, 2, KD, DE])
        odn = at("odn", 2 * KD * DE * 4, [P, 2, D])
        oxT = at("oxT", a_m, [P, KD, C])
        oaT = at("oaT", a_m + KD * C * 4, [P, 2, C])
        oslots = at("oslots", a_m + KD * C * 4 + 2 * C * 4 + 64, [P, NITEM, 2], U32)
        yk = at("yk", 0, [P, Q, 2, D])
        fnb = at("fnb", 2 * Q * D * 4, [P, D])
        fsq = at("fsq", (2 * Q + 1) * D * 4, [P, 2, D])

        PS = ctx.enter_context(nc.psum_tensor("PS", [P, 8, 512], F32))
        B_BU = 4

        raw_in = [sem(f"raw_in{s}") for s in range(RAW)]
        hi_done, lo_done, unit_used = sem("hi_done"), sem("lo_done"), sem("unit_used")
        dve_read = sem("dve_read")
        sig_done = sem("sig_done")
        x_in = [sem(f"x_in{q}") for q in range(Q)]
        prm_in, b_in, c_in, cv_in, wr_in = sem("prm_in"), sem("b_in"), sem("c_in"), sem("cv_in"), sem("wr_in")
        pl = sem("pl")
        idn = sem("idn")
        far_in = sem("far_in")
        tab_ok = sem("tab_ok")
        d_s5 = sem("d_s5")
        d_cc = sem("d_cc")
        d_in = sem("d_in")
        a_in_ = sem("a_in_")
        ss_done, rs_done, xn_done = sem("ss_done"), sem("rs_done"), sem("xn_done")
        xtr = sem("xtr")
        uh_done, ul_done = sem("uh_done"), sem("ul_done")
        ptr = sem("ptr")
        ptr_read = sem("ptr_read")
        a_mth = sem("a_mth")
        d_mth = sem("d_mth")
        s5_par = sem("s5_par")
        t_done, th_done, tl_done = sem("t_done"), sem("th_done"), sem("tl_done")
        cpy_done = sem("cpy_done")
        bu_done, bu_read = sem("bu_done"), sem("bu_read")
        cf_done = sem("cf_done")
        loc = sem("loc")
        loc_done = sem("loc_done")
        cor_done = sem("cor_done")
        y_done, y_read = sem("y_done"), sem("y_read")
        ysq, ysg = sem("ysq"), sem("ysg")
        ys1 = sem("ys1")
        yw = sem("yw")
        gel_done = sem("gel_done")
        yh_done, yl_done = sem("yh_done"), sem("yl_done")
        gp_done, gh_done, gl_done = sem("gp_done"), sem("gh_done"), sem("gl_done")
        mh_done, ml_done = sem("mh_done"), sem("ml_done")
        out_in = sem("out_in")
        xt2_in = sem("xt2_in")
        hT_done, htr, htk_done = sem("hT_done"), sem("htr"), sem("htk_done")
        hrow = [sem("hrow0"), sem("hrow1")]
        res_done, xst_done, wr_done, mg_done = sem("res_done"), sem("xst_done"), sem("wr_done"), sem("mg_done")
        ldx_done, bb_done, ctz, zl_done, f_sq = (sem("ldx_done"), sem("bb_done"), sem("ctz"), sem("zl_done"),
                                                 sem("f_sq"))
        pst = sem("pst")
        xgz = sem("xgz")
        g2_in = sem("g2_in")
        h_ss, h_rs = sem("h_ss"), sem("h_rs")
        rn_done = sem("rn_done")
        g_done = sem("g_done")
        v_done, v_out = sem("v_done"), sem("v_out")
        r_exp, r_arg = sem("r_exp"), sem("r_arg")
        rdc = sem("rdc")
        cst = sem("cst")
        es_done, pos_done = sem("es_done"), sem("pos_done")
        oc_done, slp_done = sem("oc_done"), sem("slp_done")
        sl_done = sem("sl_done")
        rt_done = sem("rt_done")
        rg_done = sem("rg_done")
        pad_done = sem("pad_done")
        sc_out = [sem(f"sc_out{n}") for n in range(8)]
        m_in = [sem(f"m_in{s}") for s in range(MRAW)]
        mhi, mlo = sem("mhi"), sem("mlo")
        gu_half, gu_full, dn_done = sem("gu_half"), sem("gu_full"), sem("dn_done")
        ix_done = sem("ix_done")
        xg_in = sem("xg_in")
        xg_tr = sem("xg_tr")
        xh_done, xl_done = sem("xh_done"), sem("xl_done")
        silu_done, am_done, a_tr, ah_done, al_done = (sem("silu_done"), sem("am_done"), sem("a_tr"),
                                                      sem("ah_done"), sem("al_done"))
        yo_done, yo_out = sem("yo_done"), sem("yo_out")
        o_w, o_ix, o_x, o_tr, o_tc, o_gu, o_si, o_am, o_at, o_ac, o_dn, o_ye, o_y = [
            sem("ovf_" + n) for n in "w ix x tr tc gu si am at ac dn ye y".split()]
        osl_in = sem("osl_in")
        yk_in = [sem(f"yk_in{q}") for q in range(Q)]
        fn_in = sem("fn_in")
        f_ss, f_add, f_rs, f_out, f_st = sem("f_ss"), sem("f_add"), sem("f_rs"), sem("f_out"), sem("f_st")
        f_nrm = sem("f_nrm")
        f_rc, f_last = sem("f_rc"), sem("f_last")
        fch = sem("fch")

        def ge(eng, s, v):
            if not (isinstance(v, int) and v <= 0):
                eng.wait_ge(s, v)

        class Own:

            def __init__(self, eng, s, start=0):
                self.eng, self.s, self.n, self.base = eng, s, 0, start

            def __call__(self, ins):
                ins.then_inc(self.s, 1)
                self.n += 1
                self.eng.wait_ge(self.s, self.base + self.n)

        n_xs = 0
        n_cv = n_xs + 2 * KH // 2
        n_xb = n_cv + 4 * KH // 2
        n_ga = n_xb + 2 * KH // 2
        n_gl = n_ga + 3 * KD // 2
        n_gb = n_gl + KH // 2
        n_wo = n_gb + 3 * KD // 2
        g_cv, g_xb = KH // 2, 3 * KH // 2
        g_ga = g_xb + KH // 2
        g_gl = g_ga + KD
        g_gb = g_gl + KH // 2
        NH2, ND2 = KH // 2, KD // 2
        S5_AT = dict(zip((n_cv + 8, n_cv + 13, n_xb + 2, n_ga, n_ga + 6, n_ga + 11, n_ga + 16, n_ga + 21),
                         range(KH)))
        PART_AT = {u - 3 + x: (ft, x) for u, ft in S5_AT.items() for x in range(4)}

        w_in_v = w_in[0].rearrange("(k p) n -> p k n", p=P)
        w_glu_v = w_glu[0].rearrange("(k p) n -> p k n", p=P)
        w_co_v = w_co[0].rearrange("(k p) n -> p k n", p=P)
        w_so_v = w_so[0].rearrange("(k p) n -> p k n", p=P)
        w_o_v = w_o[0].rearrange("(k p) n -> p k n", p=P)
        w_gate_v = w_gate[0].rearrange("e (k p) n -> e p k n", p=P)
        w_up_v = w_up[0].rearrange("e (k p) n -> e p k n", p=P)
        w_down_v = w_down[0].rearrange("e (k p) n -> e p k n", p=P)

        def rows_of(j, prompt, sample, first):
            p0 = (j % JQ) * NCH
            got = [(p0 + 1, NPC - 1, prompt.rearrange("(c j) d -> j c d", j=L)[j]),
                   (p0 + NPC, NB, sample[:, j, :])]
            if first is not None:
                got.append((p0, 1, first[j:j + 1, :]))
            return got

        block = ctx.enter_context(nc.Block())

        def bcast(v, n):
            return v.rearrange("(a d) -> a d", a=1).to_broadcast([P, n])

        Q_ORDER = (0, 1, 3, 2)

        def load_rows(eng, j0, j1, dst, s):
            for j in range(j0, j1):
                for p0, n, src in rows_of(j, x_prompt[0], x_sample, meta):
                    eng.dma_start(dst[p0:p0 + n, j // JQ, :], src).then_inc(s, 16)

        @block.sync
        def _(sp):
            for q in range(Q - 1):
                load_rows(sp, q * JQ, (q + 1) * JQ, xt, x_in[q])

            slot = [0]

            def load(n, view, k0, col):
                s = slot[0] % RAW
                slot[0] += 1
                ge(sp, lo_done, n - RAW + 1)
                sp.dma_start(raw[:, s, :].rearrange("p (k c) -> p k c", k=UK),
                             view[:, k0:k0 + UK, bass.ds(col * UW, UW)]).then_inc(raw_in[s], 16)

            for g in range(NH2):
                load(n_xs + 2 * g, w_in_v, 0, g + XS)
                load(n_xs + 2 * g + 1, w_in_v, UK, g + XS)
                if g == 1:
                    for c, src in enumerate((b_re, b_im)):
                        sp.dma_start(bnat[:, c], src[0].rearrange("(s g) p h -> (g p) s h", g=2)).then_inc(b_in, 16)
                    for c, src in enumerate((c_re, c_im)):
                        for d in range(2):
                            sp.dma_start(crow[:, c, :, d * NP_:(d + 1) * NP_],
                                          src[0].rearrange("(m g) h p -> (g h) m p", g=P // NH)).then_inc(c_in, 16)
                    for c, src in enumerate((state_re, state_im)):
                        sp.dma_start(srow[:, c], src[0].rearrange("b (s g) p -> (b s) (g p)", g=2)
                                      .rearrange("(m r) x -> r m x", m=2)).then_inc(c_in, 16)
            with sp.Fori(0, NH2) as i:
                for c, blk in enumerate((XC, XV)):
                    load(n_cv + 4 * i + 2 * c, w_in_v, 0, i + blk)
                    load(n_cv + 4 * i + 2 * c + 1, w_in_v, UK, i + blk)
            with sp.Fori(0, NH2) as i:
                load(n_xb + 2 * i, w_in_v, 0, i + XB)
                load(n_xb + 2 * i + 1, w_in_v, UK, i + XB)
            with sp.Fori(0, ND2 // 2) as i:
                for h in range(2):
                    load(n_ga + 6 * i + 3 * h, w_in_v, 0, 2 * i + h + GA)
                    load(n_ga + 6 * i + 3 * h + 1, w_in_v, UK, 2 * i + h + GA)
                    load(n_ga + 6 * i + 3 * h + 2, w_co_v, 0, 2 * i + h)
            with sp.Fori(0, NH2 // 2) as i:
                for h in range(2):
                    load(n_gl + 2 * i + h, w_glu_v, 0, 2 * i + h)
            with sp.Fori(0, ND2 // 2) as i:
                for h in range(2):
                    load(n_gb + 6 * i + 3 * h, w_in_v, 0, 2 * i + h + GB)
                    load(n_gb + 6 * i + 3 * h + 1, w_in_v, UK, 2 * i + h + GB)
                    load(n_gb + 6 * i + 3 * h + 2, w_so_v, 0, 2 * i + h)
            with sp.Fori(0, ND2) as i:
                load(n_wo + 2 * i, w_o_v, 0, i)
                load(n_wo + 2 * i + 1, w_o_v, UK, i)

            cursor = [0]

            def mload(n, src, k):
                s = cursor[0] % MRAW
                cursor[0] += 1
                if isinstance(n, int) and n == MRAW // 2:
                    sp.wait_ge(htr, ND2)
                if isinstance(n, int) and n == MRAW:
                    for q in range(Q):
                        sp.wait_ge(v_done, q + 1)
                        sp.dma_start(vbuf[q * TQ:(q + 1) * TQ, :], xt2[0:TQ, q, :]).then_inc(v_out, 16)
                ge(sp, mlo, n - MRAW + 1)
                sp.dma_start(mraw[s].rearrange("p (k c) -> p k c", k=k), src).then_inc(m_in[s], 16)

            def load_gu(n, e, half):
                mload(n, w_gate_v[e][:, half * UK:(half + 1) * UK, :], UK)
                mload(n + 1, w_up_v[e][:, half * UK:(half + 1) * UK, :], UK)

            def load_d(n, e):
                for h in range(2):
                    mload(n + h, w_down_v[e][:, :, h * (D // 2):(h + 1) * (D // 2)], 2)

            sp.wait_ge(ml_done, 4)
            load_gu(0, 0, 0)
            load_gu(2, 0, 1)
            load_gu(4, 1, 0)
            load_gu(6, 1, 1)

            def rest(n, e):
                load_d(n, e - 1)
                load_gu(n + 2, e + 1, 0)
                load_gu(n + 4, e + 1, 1)

            rest(8, 1)
            with sp.Fori(2, NE - 1) as e:
                rest(6 * e + 2, e)
            load_d(6 * NE - 4, NE - 2)
            load_d(6 * NE - 2, NE - 1)

            sp.wait_ge(mlo, 6 * NE)
            sp.dma_start(fnb[:, :], bcast(final_norm, D)).then_inc(fn_in, 16)

            sp.wait_ge(yo_out, 16 * NE)
            sp.wait_ge(rt_done, 1)
            over = sp.value_load(flag[0:1, 0:1], min_val=0, max_val=1)
            with sp.If(over > 0):
                for x in range(8):
                    sp.wait_ge(sc_out[x], 16)
                sp.dma_start(oslots[0:C, :, :], tab.rearrange("(s i) v -> s i v", i=NITEM)).then_inc(osl_in, 16)
                for ps in range(1, MORE):
                    with sp.Fori(0, NE) as e:
                        n = e + (ps - 1) * NE
                        sp.wait_ge(o_ye, n + 1)
                        sp.dma_start(ogu[:, 0], w_gate_v[e]).then_inc(o_w, 16)
                        sp.dma_start(ogu[:, 1], w_up_v[e]).then_inc(o_w, 16)
                        sp.dma_start(odn[:, :, :], w_down_v[e]).then_inc(o_w, 16)
                sp.wait_ge(o_y, 16 * (MORE - 1) * NE)
            sp.nop()

            yv = ybuf.rearrange("(t k) d -> t k d", k=2)

            def store(q):
                if q < Q - 1:
                    sp.wait_ge(f_out, q + 1)
                else:
                    sp.wait_ge(f_last, 1)
                for j in range(q * JQ, (q + 1) * JQ):
                    for p0, n, dst in rows_of(j, y_prompt[0], y_sample, None):
                        sp.dma_start(dst, htok[p0:p0 + n, q, :]).then_inc(f_st, 16)

            for q in range(Q):
                sp.dma_start(yk[0:TQ, q], yv[q * TQ:(q + 1) * TQ]).then_inc(yk_in[q], 16)
            for q in range(Q):
                store(q)
            sp.wait_ge(f_st, 16 * 2 * L)
            sp.wait_ge(out_in, 16 * 10)

        @block.scalar
        def _(act):
            for r0, src in ((0, norm1[0].rearrange("(k p) -> k p", p=P)),
                            (O_N2, norm2[0].rearrange("(k p) -> k p", p=P)),
                            (O_CW, conv_w[0].rearrange("w (k p) -> (w k) p", p=P)),
                            (O_D, ssm_d[0].rearrange("(k p) -> k p", p=P)),
                            (O_LR, lam_re[0].rearrange("(s g) p -> s (g p)", g=2)),
                            (O_LI, lam_im[0].rearrange("(s g) p -> s (g p)", g=2))):
                act.dma_start(vrow[r0:r0 + src.shape[0], :], src).then_inc(prm_in, 16)
            act.dma_start(ldrow[0:NST, :], log_dt[0].rearrange("(s g) -> s g", g=2)).then_inc(prm_in, 16)
            slot = [0]

            def hi(n):
                s = slot[0] % RAW
                slot[0] += 1
                act.wait_ge(raw_in[s], (n - s) * 8 + 16)
                ge(act, unit_used, n - SPL + 1)
                act.activation(spH[:, s, :], raw[:, s, :], ACT.Copy).then_inc(hi_done, 1)
                if isinstance(n, int) and n - 1 in S5_AT:
                    ft = S5_AT[n - 1]
                    if ft + 2 < KH:
                        bu_prepare(ft + 2, ft % 2)
                        bu_read_(ft + 2, ft % 2)
                    gelu_act(ft)

            def bu_prepare(ft, par):
                ge(act, bu_done, 8 * (ft - 1))
                act.activation(btc[:, par], BT[:, ft], ACT.Copy).then_inc(cpy_done, 1)
                act.activation(usc[:, par], xs[:, ft], ACT.Copy).then_inc(cpy_done, 1)
                ge(act, y_done, ft - 1)
                for half in range(2):
                    p0, c0 = 64 * half, NH * half
                    act.activation(ctc[p0:p0 + 64, par].rearrange("p c (s h) -> p c s h", h=32)[:, :, :, c0:c0 + NH],
                                   CT[p0:p0 + 64, ft], ACT.Copy).then_inc(cpy_done, 1)

            def bu_read_(ft, par):
                for s in range(SPF):
                    for c in range(2):
                        act.wait_ge(bu_done, ft * 8 + 2 * s + c + 1)
                        act.activation(st[:, par, :, c, s, :],
                                       PS[:, B_BU + (2 * s + c) % 3, 0:T].rearrange("p (j h) -> p j h", h=NCH),
                                       ACT.Copy).then_inc(bu_read, 1)

            def gelu_act(ft):
                act.wait_ge(y_read, ft + 1)
                ge(act, gel_done, ft)
                act.activation(gt[:, :], xs[:, ft], ACT.Square).then_inc(ysq, 1)
                act.wait_ge(yw, ft + 1)
                act.activation(gt[:, :], gt[:, :], ACT.Sigmoid, scale=1.5957691216057308).then_inc(ysg, 1)

            for x, q in enumerate(Q_ORDER):
                act.wait_ge(x_in[q], 16 * 3 * JQ)
                if x:
                    act.wait_ge(ss_done, x)
                act.activation(sq[0:TQ, :], xt[0:TQ, q, :], ACT.Square,
                               accum_out=stat[0:TQ, 0, q:q + 1]).then_inc(ss_done, 1)
                act.wait_ge(rs_done, x + 1)
                act.activation(stat[0:TQ, 2, q:q + 1], stat[0:TQ, 1, q:q + 1], ACT.Sqrt).then_inc(a_in_, 1)
            hi(0)
            hi(1)
            for k in range(KD):
                if k == 0:
                    act.wait_ge(ptr_read, 1)
                act.wait_ge(xtr, k + 1)
                act.activation(uHL[:, 0, k, :], PS[:, k % 4, 0:T], ACT.Copy,
                               scale=vecs[:, k:k + 1]).then_inc(uh_done, 1)

            act.wait_ge(d_mth, 1)
            act.activation(sm[:, 1, :], sm[:, 0, :], ACT.Exp).then_inc(a_mth, 1)
            act.wait_ge(d_mth, 2)
            act.activation(sm[:, 4, :], sm[:, 2, :], ACT.Exp).then_inc(a_mth, 1)
            act.wait_ge(d_mth, 3)
            act.activation(sm[:, 10, :], sm[:, 7, :], ACT.Sin).then_inc(a_mth, 1)
            act.activation(sm[:, 11, :], sm[:, 9, :], ACT.Sin).then_inc(a_mth, 1)
            for g in range(NH2):
                hi(n_xs + 2 * g + 2)
                hi(n_xs + 2 * g + 3)
            act.wait_ge(dve_read, NH2)
            act.wait_ge(s5_par, 1)
            act.wait_ge(ctz, 1)
            act.wait_ge(tab_ok, 16)
            for ft in range(2):
                bu_prepare(ft, ft)
                bu_read_(ft, ft)
            act.dma_start(cvrow[0:2 * NB, :], state_conv[0].rearrange("b k d -> (b k) d")).then_inc(cv_in, 16)
            for n in range(n_cv + 2, n_xb + 2):
                hi(n)
            for g in range(NH2):
                hi(n_xb + 2 * g + 2)
                if g == 1:
                    act.wait_ge(ptr_read, 13)
                    for k in range(2):
                        r0 = k * (1 + NB)
                        act.dma_start(nconv_p[0, :, k, :], cvrow[r0:r0 + 1, :]).then_inc(out_in, 16)
                        act.dma_start(nconv_s[0, :, k, :], cvrow[r0 + 1:r0 + 1 + NB, :]).then_inc(out_in, 16)
                hi(n_xb + 2 * g + 3)
                act.wait_ge(t_done, g + 1)
                act.activation(tHL[:, 0, 2 * g:2 * g + 2, :], tmp[:, :, :], ACT.Copy).then_inc(th_done, 1)

            act.nop().then_inc(sig_done, 1)

            for g in range(ND2):
                n = n_ga + 3 * g
                hi(n + 2)
                act.wait_ge(unit_used, n + 2)
                ge(act, dve_read, g + g_ga)
                act.wait_ge(tl_done, NH2)
                act.activation(tmp[:, :, :], PS[:, 0:2, 0:T], ACT.Sigmoid).then_inc(sig_done, 1)
                hi(n + 3)
                if g == ND2 - 1:
                    act.wait_ge(gel_done, KH)
                    act.wait_ge(y_done, KH)
                    for c in range(2):
                        act.activation(gHL[:, 0, 4 * c:4 * c + 4, :], xs[:, 4 * c:4 * c + 4, :],
                                       ACT.Copy).then_inc(yh_done, 1)
                hi(n + 4)
            act.wait_ge(y_done, KH)
            for c0, src in ((0, w_coarse), (NEG, w_fine)):
                act.dma_start(wr[:, :, c0:c0 + src.shape[2]],
                              src[0].rearrange("(k p) n -> p k n", p=P)).then_inc(wr_in, 16)
            for g in range(NH2):
                act.wait_ge(unit_used, n_gl + g + 1)
                act.wait_ge(dve_read, g_ga + ND2)
                ge(act, gp_done, g)
                b = 2 * (g % 2)
                act.activation(tmp[:, :, :], PS[:, b:b + 2, 0:T], ACT.Sigmoid).then_inc(sig_done, 1)
                hi(n_gl + g + 2)
                act.wait_ge(gp_done, g + 1)
                act.activation(tHL[:, 0, 2 * g:2 * g + 2, :], xs[:, 2 * g:2 * g + 2, :], ACT.Copy).then_inc(gh_done, 1)
            act.wait_ge(ptr_read, 15)
            for c, (dp, ds_) in enumerate(((nre_p, nre_s), (nim_p, nim_s))):
                act.dma_start(dp[0].rearrange("b (s g) p -> (b s) (g p)", g=2), frow[0:NST, 3 * c, :]).then_inc(out_in, 16)
                rows = ds_[0].rearrange("b (s g) p -> (b s) (g p)", g=2)
                for m in range(2):
                    act.dma_start(rows[m * P:(m + 1) * P, :], frow[:, 3 * c + 1 + m, :]).then_inc(out_in, 16)

            def merged_hi(c):
                act.activation(uHL[:, 0, 4 * c:4 * c + 4, :], mrg[:, 4 * c:4 * c + 4, :], ACT.Copy).then_inc(mh_done, 1)

            def gb_so(i, last=False):
                for h in range(2):
                    n, g = n_gb + 6 * i + 3 * h, 2 * i + h
                    hi(n + 2)
                    act.wait_ge(unit_used, n + 2)
                    act.wait_ge(mg_done, g + 1)
                    act.activation(tmp[:, :, :], PS[:, 0:2, 0:T], ACT.Sigmoid).then_inc(sig_done, 1)
                    hi(n + 3)
                    if last and h == 1:
                        for c in range(3):
                            merged_hi(c)
                        act.wait_ge(mg_done, ND2 + 1)
                        merged_hi(3)
                    hi(n + 4)

            with act.Fori(0, ND2 // 2 - 1) as i:
                gb_so(i)
            gb_so(ND2 // 2 - 1, True)
            act.dma_start(g2b[:, :], bcast(norm2[0], D)).then_inc(g2_in, 16)
            act.wait_ge(out_in, 16 * 10)
            act.wait_ge(xt2_in, 16 * 3 * L)

            def squares(x, c0, c1):
                for q in range(Q):
                    ge(act, h_ss, Q * x // 4 + q)
                    act.activation(mjunk[0:TQ, 0:c1 - c0], htok[0:TQ, q, c0:c1], ACT.Square,
                                   accum_out=stat[0:TQ, x, q:q + 1]).then_inc(h_ss, 1)

            def w_o_group(i, h, tail):
                g, n = 2 * i + h, n_wo + 4 * i + 2 * h
                if not tail:
                    hi(n + 2)
                ge(act, res_done, g)
                act.activation(xst[0:TQ], xt2[0:TQ, :, bass.ds(g * UW, UW)], ACT.Copy).then_inc(xst_done, 1)
                if tail:
                    act.wait_ge(htk_done, 2 * SQ1 // UW)
                    squares(0, 0, SQ1)
                act.wait_ge(res_done, g + 1)
                ge(act, htr, g - 1)
                act.activation(hT[:, h], PS[:, 2 * h:2 * h + 2, 0:T], ACT.Copy).then_inc(hT_done, 1)
                if not tail:
                    hi(n + 3)

            w_o_group(0, 0, False)
            w_o_group(0, 1, False)
            with act.Fori(1, ND2 // 2 - 1) as i:
                w_o_group(i, 0, False)
                w_o_group(i, 1, False)
            w_o_group(ND2 // 2 - 1, 0, False)
            w_o_group(ND2 // 2 - 1, 1, True)

            act.wait_ge(htk_done, 2 * ND2)
            squares(4, SQ1, D)
            act.wait_ge(h_rs, 1)
            act.activation(stat[0:TQ, 2, :], stat[0:TQ, 1, :], ACT.Sqrt).then_inc(a_in_, 1)
            act.wait_ge(rn_done, 1)
            act.wait_ge(g_done, ND2)
            for q in range(Q):
                act.activation(xt2[0:TQ, q, :], xt2[0:TQ, q, :], ACT.Copy, scale=stat[0:TQ, 3, q:q + 1]) \
                    .then_inc(v_done, 1)
            act.wait_ge(r_arg, 1)
            act.activation(cex[0:TQ], cex[0:TQ], ACT.Exp).then_inc(r_exp, 1)
            act.wait_ge(r_arg, 2)
            act.activation(rs[0:TQ, 3, :], rs[0:TQ, 2, :], ACT.Exp).then_inc(r_exp, 1)

            cursor = [0]

            def mhi_(n0, e, s, free=None):
                r = cursor[0] % MRAW
                cursor[0] += 1
                assert n0 % MRAW == r
                act.wait_ge(m_in[r], e * 16 + 16 * ((n0 - r) // MRAW + 1))
                if free is not None:
                    ge(act, *free)
                act.activation(mH[s], mraw[r], ACT.Copy).then_inc(mhi, 1)

            def xh(e):
                for b in range(4):
                    act.wait_ge(xg_tr, e * 4 + b + 1)
                    act.activation(xTH[:, 4 * b:4 * b + 4, 0:C],
                                   PS[:, 2 + b % 2, 0:4 * CM].rearrange("p (k c) -> p k c", k=4)[:, :, 0:C],
                                   ACT.Copy).then_inc(xh_done, 1)

            def ah(e):
                act.wait_ge(a_tr, e + 1)
                ge(act, dn_done, e)
                act.activation(aTH[:, :, 0:C], PS[:, 1, 0:2 * CM].rearrange("p (k c) -> p k c", k=2)[:, :, 0:C],
                               ACT.Copy).then_inc(ah_done, 1)

            def y_out(e):
                act.wait_ge(dn_done, e + 1)
                ge(act, yo_out, e * 16)
                act.activation(yo[0:C, :].rearrange("p (n c) -> p n c", n=4), PS[0:C, 4:8, :],
                               ACT.Copy).then_inc(yo_done, 1)

            def silu(e):
                act.wait_ge(gu_full, e + 1)
                ge(act, am_done, e)
                act.activation(sg[0:C, :], PS[0:C, 0, 0:DE], ACT.Silu).then_inc(silu_done, 1)

            act.wait_ge(htr, ND2)
            for s in range(4):
                mhi_(s, 0, s)
            xh(0)

            def body(e, first, second, last):
                if not first:
                    ah(e - 1)
                    if second:
                        act.wait_ge(v_out, 16 * Q)
                    for h in range(2):
                        mhi_(2 + h, e, 4 + h, (dn_done, e - 1))
                if not (first or second):
                    y_out(e - 2)
                n0 = 4
                if not last:
                    for h in range(2):
                        mhi_(n0 + h, e, h, (gu_half, e + 1))
                silu(e)
                if not last:
                    xh(e + 1)
                    for h in range(2):
                        mhi_(n0 + 2 + h, e, 2 + h, None)

            body(0, True, False, False)
            body(1, False, True, False)
            with act.Fori(2, NE - 1) as e:
                body(e, False, False, False)
            body(NE - 1, False, False, True)
            ah(NE - 1)
            for h in range(2):
                mhi_(4 + h, NE - 1, 4 + h, (dn_done, NE - 1))
            y_out(NE - 2)
            y_out(NE - 1)

            act.wait_ge(yo_out, 16 * NE)
            over = act.value_load(flag[0:1, 0:1], min_val=0, max_val=1)
            with act.If(over > 0):
                act.nop().then_inc(o_ye, 1)
                with act.Fori(0, (MORE - 1) * NE) as n:
                    act.wait_ge(o_tr, n + 1)
                    for b in range(4):
                        ins = act.activation(oxT[:, 4 * b:4 * b + 4, :],
                                             PS[:, 2 + b, 0:4 * CM].rearrange("p (k c) -> p k c", k=4)[:, :, 0:C],
                                             ACT.Copy)
                    ins.then_inc(o_tc, 1)
                    act.wait_ge(o_gu, n + 1)
                    act.activation(sg[0:C, :], PS[0:C, 0, 0:DE], ACT.Silu).then_inc(o_si, 1)
                    act.wait_ge(o_at, n + 1)
                    act.activation(oaT[:, :, :], PS[:, 1, 0:2 * CM].rearrange("p (k c) -> p k c", k=2)[:, :, 0:C],
                                   ACT.Copy).then_inc(o_ac, 1)
                    act.wait_ge(o_dn, n + 1)
                    act.activation(yo[0:C, :].rearrange("p (n c) -> p n c", n=4), PS[0:C, 4:8, :],
                                   ACT.Copy).then_inc(o_ye, 1)
            act.nop()

            for q in range(Q):
                act.wait_ge(f_add, q + 1)
                if q:
                    act.wait_ge(f_ss, q)
                act.activation(fsq[0:TQ, q % 2, :], htok[0:TQ, q, :], ACT.Square,
                               accum_out=stat[0:TQ, 4, q:q + 1]).then_inc(f_ss, 1)
                act.wait_ge(f_rs, q + 1)
                act.activation(stat[0:TQ, 6, q:q + 1], stat[0:TQ, 5, q:q + 1], ACT.Sqrt).then_inc(f_sq, 1)
                if q < Q - 1:
                    act.wait_ge(f_rc, q + 1)
                    act.activation(htok[0:TQ, q, :], htok[0:TQ, q, :], ACT.Copy,
                                   scale=stat[0:TQ, 7, q:q + 1]).then_inc(f_nrm, 1)

        @block.tensor
        def _(pe):
            PT = (spH, spL)
            batch = [0]

            def transposes(pairs, wait_batch=True):
                k = batch[0]
                batch[0] += 1
                if wait_batch:
                    ge(pe, ptr_read, k - 1)
                b = 6 + k % 2
                for c0, src in pairs:
                    rows, cols = src.shape[0], src.shape[1]
                    ins = pe.transpose(PS[0:cols, b, c0:c0 + rows], src, ident[0:rows, 0:rows])
                ins.then_inc(ptr, 1)

            pe.wait_ge(idn, 2)
            pe.wait_ge(prm_in, 16 * 7)
            pe.wait_ge(ldx_done, 1)
            transposes([(0, vrow[:, :]), (P, ldx[0:NST, :])])
            for k in range(KD):
                if k == 0:
                    pe.wait_ge(xn_done, Q)
                ge(pe, ul_done, k - 3)
                for q in range(Q):
                    ins = pe.transpose(PS[:, k % 4, q * TQ:(q + 1) * TQ], xt[0:TQ, q, k * P:(k + 1) * P],
                                       ident[0:TQ, 0:TQ])
                ins.then_inc(xtr, 1)
            pe.wait_ge(ul_done, KD)

            slot = [0]

            def products(n, b, rhs, k0, first, last):
                s = slot[0] % SPL
                slot[0] += 1
                if isinstance(n, int) and n in S5_AT:
                    ft = S5_AT[n]
                    if ft in (2, 3):
                        pe.wait_ge(ptr_read, batch[0])
                    y_s5(ft, ft % 2)
                    if ft + 2 < KH:
                        bu(ft + 2, ft % 2)
                pe.wait_ge(lo_done, n + 1)
                for m in range(2):
                    for k in range(UK):
                        for w, a in PASSES:
                            ins = pe.matmul(PS[:, b + m, 0:T], PT[w][:, s, k * UW + m * P:k * UW + (m + 1) * P],
                                            rhs[:, a, k0 + k, :], start=first and k == 0 and (w, a) == (0, 0),
                                            stop=last and k == UK - 1 and (w, a) == PASSES[-1])
                ins.then_inc(unit_used, 1)

            def group(n, b, rhs, units=2):
                for u in range(units):
                    products(n + u, b, rhs, u * UK, u == 0, u == units - 1)

            def bu(ft, par):
                pe.wait_ge(cpy_done, ft * 4 + 2)
                for s in range(SPF):
                    for c in range(2):
                        m = 2 * s + c
                        if m >= 3:
                            pe.wait_ge(bu_read, ft * 8 + m - 2)
                        elif m == 0:
                            ge(pe, bu_read, ft * 8)
                        pe.matmul(PS[:, B_BU + m % 3, 0:T], btc[32 * s:32 * s + 32, par, c, :],
                                  usc[32 * s:32 * s + 32, par, :], start=True, stop=True).then_inc(bu_done, 1)

            def y_s5(ft, par):
                pe.wait_ge(cor_done, ft + 1)
                pe.wait_ge(cpy_done, ft * 4 + 4)
                ge(pe, y_read, ft)
                for s in range(SPF):
                    for c in range(2):
                        ins = pe.matmul(PS[32 * s:32 * s + 32, 7, 0:T], ctc[:, par, c, 32 * s:32 * s + 32],
                                        st[:, par, :, c, s, :], start=c == 0, stop=c == 1,
                                        tile_position=(0, 32 * s))
                ins.then_inc(y_done, 1)

            group(n_xs, 0, uHL)
            group(n_xs + 2, 2, uHL)
            pe.wait_ge(bb_done, 1)
            for c in range(2):
                for b in range(2):
                    transposes([(P * f, bbd[:, c, SPF * (4 * b + f):SPF * (4 * b + f + 1), :]
                                 .rearrange("p s x -> p (s x)")) for f in range(4)])
            pe.wait_ge(c_in, 16 * 6)
            for c in range(2):
                for b in range(2):
                    transposes([(P * f, crow[:, c, 4 * b + f, :]) for f in range(4)])
            transposes([(P * (2 * c + m), srow[:, c, m, :]) for c in range(2) for m in range(2)])
            for g in range(2, NH2):
                ge(pe, dve_read, g - 1)
                group(n_xs + 2 * g, 2 * (g % 2), uHL)
            pe.wait_ge(ptr_read, batch[0])
            pe.wait_ge(ctz, 1)
            for ft in range(2):
                bu(ft, ft)
            for i in range(NH2):
                for c in range(2):
                    pe.wait_ge(dve_read, 2 * i + g_cv + c - 1)
                    group(n_cv + 4 * i + 2 * c, 2 * c, uHL)
            pe.wait_ge(cv_in, 16)
            pe.wait_ge(bu_read, 32)
            pe.wait_ge(y_read, 2)
            transposes([(2 * NB * f, cvrow[0:2 * NB, P * f:P * (f + 1)]) for f in range(KH)])
            for g in range(NH2):
                ge(pe, dve_read, g_xb + g - 1)
                group(n_xb + 2 * g, 2 * (g % 2), uHL)
                if g == 0:
                    pe.wait_ge(zl_done, 1)
                    for b in range(2):
                        transposes([(P * f, zl[:, 4 * b + f].rearrange("p k b -> p (k b)")) for f in range(4)])

            for g in range(ND2):
                n = n_ga + 3 * g
                pe.wait_ge(dve_read, g + g_ga - 1)
                if g:
                    pe.wait_ge(sig_done, g + 1)
                group(n, 0, uHL)
                pe.wait_ge(dve_read, g + g_ga)
                ge(pe, tl_done, NH2)
                group(n + 2, 2, tHL, 1)
            pe.wait_ge(y_read, KH)
            rows = [src for c in range(2) for src in
                    (fin[:, c, 0, :], fin[:, c, 1:5, :].rearrange("p b s -> p (b s)"),
                     fin[:, c, 5:9, :].rearrange("p b s -> p (b s)"))]
            transposes([(P * x, src) for x, src in enumerate(rows[:4])])
            transposes([(P * x, src) for x, src in enumerate(rows[4:])])
            for g in range(NH2):
                if g == 0:
                    pe.wait_ge(yl_done, 2)
                    pe.wait_ge(sig_done, ND2 + 1)
                elif g == 1:
                    pe.wait_ge(dve_read, g_ga + ND2)
                else:
                    pe.wait_ge(sig_done, ND2 + g)
                group(n_gl + g, 2 * (g % 2), gHL, 1)
            with pe.Fori(0, ND2 // 2) as i:
                for h in range(2):
                    n, g = n_gb + 6 * i + 3 * h, 2 * i + h
                    pe.wait_ge(sig_done, g + ND2 + NH2 + 1)
                    group(n, 0, uHL)
                    pe.wait_ge(dve_read, g + g_ga + ND2)
                    ge(pe, gl_done, NH2)
                    group(n + 2, 2, tHL, 1)

            def after(g, h, first, last=False):
                pe.wait_ge(hT_done, g + 1)
                for m in range(2):
                    ge(pe, htk_done, 2 * g + m - 1)
                    for q in range(Q):
                        ins = pe.transpose(PS[0:TQ, 4 + m, q * P:(q + 1) * P], hT[:, h, m, q * TQ:(q + 1) * TQ],
                                           ident[:, :])
                    ins.then_inc(hrow[m], 1)
                for m in range(2):
                    for q in range(Q):
                        ins = pe.matmul(PS[0:TQ, 6, q * NR:(q + 1) * NR], hT[:, h, m, q * TQ:(q + 1) * TQ],
                                        wr[:, 2 * g + m, :], start=first and m == 0 and q == 0, stop=last and m == 1,
                                        skip_group_check=True)
                ins.then_inc(htr, 1)

            def w_o_group(i, h, first):
                g, n = 2 * i + h, n_wo + 4 * i + 2 * h
                if isinstance(g, int) and g == 0:
                    pe.wait_ge(sig_done, 2 * ND2 + NH2 + 1)
                    pe.wait_ge(ml_done, 2)
                elif isinstance(g, int) and g == 1:
                    pe.wait_ge(dve_read, g_ga + 2 * ND2)
                else:
                    pe.wait_ge(hT_done, g - 1)
                products(n, 2 * h, uHL, 0, True, False)
                if isinstance(g, int) and g == 0:
                    pe.wait_ge(ml_done, 4)
                    pe.wait_ge(wr_done, 1)
                else:
                    after(g - 1, 1 - h, isinstance(g, int) and g == 1)
                products(n + 1, 2 * h, uHL, UK, False, True)
                pe.wait_ge(xst_done, g + 1)
                for m in range(2):
                    for q in range(Q):
                        ins = pe.matmul(PS[:, 2 * h + m, q * TQ:(q + 1) * TQ], xst[0:TQ, q, m * P:(m + 1) * P],
                                        ident[0:TQ, 0:TQ], start=False, stop=True, skip_group_check=True)
                ins.then_inc(res_done, 1)

            w_o_group(0, 0, True)
            w_o_group(0, 1, False)
            with pe.Fori(1, ND2 // 2) as i:
                w_o_group(i, 0, False)
                w_o_group(i, 1, False)
            after(ND2 - 1, 1, False, True)

            pe.wait_ge(cst, 5)
            pe.wait_ge(es_done, 1)
            pe.matmul(PS[0:TQ, 7, 0:NE], lst[0:TQ, 0:TQ], esum[0:TQ, 0, :], start=True, stop=True,
                      skip_group_check=True)
            for r in range(Q):
                ins = pe.matmul(PS[0:TQ, 7, (r + 1) * NE:(Q + 1) * NE], one[0:TQ, 0:TQ],
                                esum[0:TQ, r, :].unsqueeze(1).to_broadcast([TQ, Q - r, NE]), start=False,
                                stop=r == Q - 1, skip_group_check=True)
                if r < Q - 1:
                    pe.matmul(PS[0:TQ, 7, (r + 1) * NE:(r + 2) * NE], lst[0:TQ, 0:TQ], esum[0:TQ, r + 1, :],
                              start=False, stop=True, skip_group_check=True)
            ins.then_inc(pos_done, 1)
            pe.wait_ge(oc_done, 1)
            for m in range(2 * Q):
                ins = pe.matmul(PS[0:C, 6, 0:2 * NE], oc[0:TQ, m // Q, m % Q, :],
                                etok[0:TQ, m // Q, m % Q].rearrange("p e v -> p (e v)"), start=m == 0, stop=m == 2 * Q - 1)
            ins.then_inc(slp_done, 1)

            MG, MD = (mHg, mLg), (mHd, mLd)
            XT, AT = (xTH, xTL), (aTH, aTL)

            def xt_(e):
                pe.wait_ge(xg_in, e * 16 + 16)
                for b in range(4):
                    ge(pe, xl_done, 4 * e + b - 1)
                    for k in range(4):
                        ins = pe.transpose(PS[:, 2 + b % 2, k * CM:(k + 1) * CM],
                                           xg[0:CM, (4 * b + k) * P:(4 * b + k + 1) * P], ident[0:CM, 0:CM])
                    ins.then_inc(xg_tr, 1)

            def gate_up(e, n0):
                pe.wait_ge(xl_done, e * 4 + 4)
                ge(pe, am_done, e)
                for half in range(2):
                    pe.wait_ge(mlo, n0 + 2 * half + 2)
                    for k in range(UK):
                        for w, a in PASSES:
                            ins = pe.matmul(PS[0:CM, 0, 0:2 * DE], XT[a][:, half * UK + k, :],
                                            MG[w][:, 2 * half:2 * half + 2, k * DE:(k + 1) * DE],
                                            start=half == 0 and k == 0 and (w, a) == (0, 0),
                                            stop=half == 1 and k == UK - 1 and (w, a) == PASSES[-1])
                    ins.then_inc(gu_full if half else gu_half, 1)

            def at_(e):
                pe.wait_ge(am_done, e + 1)
                ge(pe, al_done, e)
                for k in range(2):
                    ins = pe.transpose(PS[:, 1, k * CM:(k + 1) * CM], act_[0:CM, k * P:(k + 1) * P],
                                       ident[0:CM, 0:CM])
                ins.then_inc(a_tr, 1)

            def down(e, n0):
                pe.wait_ge(al_done, e + 1)
                ge(pe, yo_done, e)
                pe.wait_ge(mlo, n0 + 2)
                for c in range(4):
                    for k in range(2):
                        for w, a in PASSES:
                            o = k * (D // 2) + (c % 2) * 512
                            ins = pe.matmul(PS[0:CM, 4 + c, :], AT[a][:, k, :], MD[w][:, c // 2, o:o + 512],
                                            start=k == 0 and (w, a) == (0, 0), stop=k == 1 and (w, a) == PASSES[-1])
                ins.then_inc(dn_done, 1)

            def body(e, n0, first, last):
                if not first:
                    at_(e - 1)
                gate_up(e, n0)
                if not last:
                    xt_(e + 1)
                if not first:
                    down(e - 1, 6 * e + 2)

            xt_(0)
            pe.wait_ge(pad_done, 5)
            body(0, 0, True, False)
            body(1, 4, False, False)
            with pe.Fori(2, NE - 1) as e:
                body(e, 6 * e - 2, False, False)
            body(NE - 1, 6 * (NE - 1) - 2, False, True)
            at_(NE - 1)
            down(NE - 1, 6 * NE - 2)

            pe.wait_ge(yo_out, 16 * NE)
            over = pe.value_load(flag[0:1, 0:1], min_val=0, max_val=1)
            with pe.If(over > 0):
                with pe.Fori(0, (MORE - 1) * NE) as n:
                    pe.wait_ge(o_x, n * 16 + 16)
                    for k in range(KD):
                        ins = pe.transpose(PS[:, 2 + k // 4, (k % 4) * CM:(k % 4 + 1) * CM],
                                           xg[0:CM, k * P:(k + 1) * P], ident[0:CM, 0:CM])
                    ins.then_inc(o_tr, 1)
                    pe.wait_ge(o_tc, n + 1)
                    pe.wait_ge(o_w, n * 48 + 48)
                    for k in range(KD):
                        ins = pe.matmul(PS[0:C, 0, 0:2 * DE], oxT[:, k, :], ogu[:, :, k, :],
                                        start=k == 0, stop=k == KD - 1)
                    ins.then_inc(o_gu, 1)
                    pe.wait_ge(o_am, n + 1)
                    for k in range(2):
                        ins = pe.transpose(PS[:, 1, k * CM:(k + 1) * CM], act_[0:CM, k * P:(k + 1) * P],
                                           ident[0:CM, 0:CM])
                    ins.then_inc(o_at, 1)
                    pe.wait_ge(o_ac, n + 1)
                    for c in range(4):
                        for k in range(2):
                            ins = pe.matmul(PS[0:C, 4 + c, :], oaT[:, k, :], odn[:, k, c * 512:(c + 1) * 512],
                                            start=k == 0, stop=k == 1)
                    ins.then_inc(o_dn, 1)
            pe.nop()

        @block.vector
        def _(dve):
            slot = [0]

            def lo(n):
                s = slot[0] % RAW
                slot[0] += 1
                dve.wait_ge(hi_done, n + 1)
                dve.tensor_tensor(spL[:, s, :], raw[:, s, :], spH[:, s, :].bitcast(F32),
                                  ALU.subtract).then_inc(lo_done, 1)
                if isinstance(n, int) and n - 1 in S5_AT:
                    y_gelu(S5_AT[n - 1])
                if isinstance(n, int) and n in PART_AT:
                    correct(*PART_AT[n])

            TT, TS = dve.tensor_tensor, dve.tensor_scalar

            def correct(ft, x):
                par = ft % 2
                cc = Own(dve, d_cc, ft * 4 * (L - 1) + 16 * x)
                shape = [P, 2, SPF, NPC - 1]
                a1 = A1[:, :, ft * SPF:(ft + 1) * SPF].unsqueeze(3).to_broadcast(shape)
                a2 = A2[:, :, ft * SPF:(ft + 1) * SPF].unsqueeze(3).to_broadcast(shape)
                view = lambda t: t.rearrange("p (c s h) -> p c s h", c=2, s=SPF)
                w1, w2, dd = view(dt1[:, :]), view(dt2[:, :]), view(dcor[:, :])
                if x == 0:
                    dve.wait_ge(loc_done, ft + 1)
                for j in range(4 * x, min(4 * x + 4, L - 1)):
                    prev = st[:, par, L - 1, :, :, 0:NPC - 1] if j == 0 else dd
                    TT(w1, prev, a1, ALU.mult).then_inc(d_cc, 1)
                    cc.n += 1
                    cc(TT(w2, prev[:, ::-1], a2, ALU.mult))
                    cc(TT(dd, w1, w2, ALU.add))
                    TT(st[:, par, j, :, :, 1:NPC], st[:, par, j, :, :, 1:NPC], dd, ALU.add).then_inc(d_cc, 1)
                    cc.n += 1
                if x == 3:
                    dve.wait_ge(d_cc, cc.base + cc.n)
                    dve.tensor_copy(fin[:, :, :, ft * SPF:(ft + 1) * SPF],
                                    st[:, par, L - 1, :, :, NPC - 1:NCH].rearrange("p c s b -> p c b s")) \
                        .then_inc(cor_done, 1)

            def y_gelu(ft):
                dve.wait_ge(y_done, ft + 1)
                dve.scalar_tensor_tensor(out=xs[:, ft], in0=xs[:, ft], scalar=vecs[:, ft + O_D:ft + O_D + 1],
                                         in1=PS[:, 7, 0:T], op0=ALU.mult, op1=ALU.add).then_inc(y_read, 1)
                dve.wait_ge(ysq, ft + 1)
                TS(gt[:, :], gt[:, :], 0.044715, 1.0, ALU.mult, ALU.add).then_inc(ys1, 1)
                dve.wait_ge(ys1, ft + 1)
                TT(gt[:, :], gt[:, :], xs[:, ft], ALU.mult).then_inc(yw, 1)
                dve.wait_ge(ysg, ft + 1)
                TT(xs[:, ft], xs[:, ft], gt[:, :], ALU.mult).then_inc(gel_done, 1)

            def newton(k, y, x, w):
                k(TT(w, y, y, ALU.mult))
                k(TT(w, w, x, ALU.mult))
                k(TS(w, w, -0.5, 1.5, ALU.mult, ALU.add))
                return TT(y, y, w, ALU.mult)

            own = Own(dve, d_in)
            dve.wait_ge(prm_in, 16 * 7)
            dve.tensor_copy(ldx[0:NST, :].rearrange("s (g p) -> s g p", g=2),
                            ldrow[0:NST, :].unsqueeze(2).to_broadcast([NST, 2, NP_])).then_inc(ldx_done, 1)
            dve.wait_ge(ptr, 1)
            dve.tensor_copy(vecs[:, :], PS[:, 6, 0:P]).then_inc(d_in, 1)
            own.n += 1
            dve.tensor_copy(sm[:, 0, :], PS[:, 6, P:P + NST]).then_inc(ptr_read, 1)
            dve.wait_ge(ptr_read, 1)
            for x, q in enumerate(Q_ORDER):
                dve.wait_ge(ss_done, x + 1)
                dve.tensor_scalar(stat[0:TQ, 1, q:q + 1], stat[0:TQ, 0, q:q + 1], 1.0 / D, EPS,
                                  ALU.mult, ALU.add).then_inc(rs_done, 1)
                dve.wait_ge(a_in_, x + 1)
                own(dve.reciprocal(stat[0:TQ, 3, q:q + 1], stat[0:TQ, 2, q:q + 1]))
                own(newton(own, stat[0:TQ, 3, q:q + 1], stat[0:TQ, 1, q:q + 1], stat[0:TQ, 8, q:q + 1]))
                dve.tensor_scalar(xt[0:TQ, q, :], xt[0:TQ, q, :], stat[0:TQ, 3, q:q + 1], None,
                                  ALU.mult).then_inc(xn_done, 1)
            lo(0)
            lo(1)
            for k in range(KD):
                dve.wait_ge(uh_done, k + 1)
                dve.scalar_tensor_tensor(out=uHL[:, 1, k, :], in0=PS[:, k % 4, 0:T], scalar=vecs[:, k:k + 1],
                                         in1=uHL[:, 0, k, :].bitcast(F32), op0=ALU.mult,
                                         op1=ALU.subtract).then_inc(ul_done, 1)

            m = Own(dve, d_s5)
            S = lambda i: sm[:, i, :]
            lr, li = vecs[:, O_LR:O_LR + NST], vecs[:, O_LI:O_LI + NST]
            dve.nop().then_inc(d_mth, 1)
            dve.wait_ge(a_mth, 1)
            m(TT(S(3), li, S(1), ALU.mult))
            TT(S(2), lr, S(1), ALU.mult).then_inc(d_mth, 1)
            m(TS(S(5), S(3), 1.0 / (2 * PI), None, ALU.mult))
            m(dve.tensor_copy(smi[:, :], S(5)))
            m(dve.tensor_copy(S(6), smi[:, :]))
            m(dve.scalar_tensor_tensor(out=S(7), in0=S(6), scalar=-TWO_PI_HI, in1=S(3), op0=ALU.mult, op1=ALU.add))
            m(dve.scalar_tensor_tensor(out=S(7), in0=S(6), scalar=-TWO_PI_LO, in1=S(7), op0=ALU.mult, op1=ALU.add))
            m(TS(S(8), S(7), PI, -2 * PI, ALU.is_gt, ALU.mult))
            m(TT(S(7), S(7), S(8), ALU.add))
            m(TS(S(8), S(7), -PI, 2 * PI, ALU.is_lt, ALU.mult))
            m(TT(S(7), S(7), S(8), ALU.add))
            m(TS(S(9), S(7), PI / 2, None, ALU.add))
            m(TS(S(8), S(9), PI, -2 * PI, ALU.is_gt, ALU.mult))
            m(TT(S(9), S(9), S(8), ALU.add))
            m(TS(S(9), S(9), PI_SAFE, -PI_SAFE, ALU.min, ALU.max))
            TS(S(7), S(7), PI_SAFE, -PI_SAFE, ALU.min, ALU.max).then_inc(d_mth, 1)
            lo(2)
            dve.wait_ge(a_mth, 4)
            m(TT(S(12), S(4), S(11), ALU.mult))
            m(TT(S(13), S(4), S(10), ALU.mult))
            def table(a1, a2):
                m(dve.tensor_copy(a1[:, 0, :], S(12)))
                m(dve.tensor_copy(a1[:, 1, :], S(12)))
                m(TS(a2[:, 0, :], S(13), -1.0, None, ALU.mult))
                m(dve.tensor_copy(a2[:, 1, :], S(13)))

            table(A1, A2)
            m(TS(S(14), S(12), 1.0, None, ALU.subtract))
            m(TT(S(15), lr, lr, ALU.mult))
            m(TT(S(16), li, li, ALU.mult))
            m(TT(S(15), S(15), S(16), ALU.add))
            m(dve.reciprocal(S(15), S(15)))
            m(TT(S(16), S(14), lr, ALU.mult))
            m(TT(S(17), S(13), li, ALU.mult))
            m(TT(S(16), S(16), S(17), ALU.add))
            m(TT(S(16), S(16), S(15), ALU.mult))
            m(TT(S(17), S(13), lr, ALU.mult))
            m(TT(S(18), S(14), li, ALU.mult))
            m(TT(S(17), S(17), S(18), ALU.subtract))
            m(TT(S(17), S(17), S(15), ALU.mult))
            lo(3)
            m(dve.memset(bbd[:, :, :, :], 0.0))
            dve.wait_ge(b_in, 32)
            kk = [S(16 + c).unsqueeze(2).to_broadcast([P, NST, NH]) for c in range(2)]
            for c, op in enumerate((ALU.subtract, ALU.add)):
                m(TT(bcm[:, :, :], bnat[:, 1 - c], kk[1], ALU.mult))
                for half in range(2):
                    p = slice(64 * half, 64 * half + 64)
                    m(TT(bbd[p, c, :, NH * half:NH * (half + 1)], bnat[p, c],
                         S(16)[p].unsqueeze(2).to_broadcast([64, NST, NH]), ALU.mult))
                for half in range(2):
                    p = slice(64 * half, 64 * half + 64)
                    m(TT(bbd[p, c, :, NH * half:NH * (half + 1)], bbd[p, c, :, NH * half:NH * (half + 1)],
                         bcm[p], op))
            dve.nop().then_inc(bb_done, 1)
            def xs_read(g):
                dve.wait_ge(unit_used, n_xs + 2 * g + 2)
                b = 2 * (g % 2)
                dve.tensor_copy(xs[:, 2 * g:2 * g + 2, :], PS[:, b:b + 2, 0:T]).then_inc(dve_read, 1)

            k = 1
            for c in range(2):
                for b in range(2):
                    dve.wait_ge(ptr, k + 1)
                    dve.tensor_copy(BT[:, 4 * b:4 * b + 4, c, :],
                                    PS[:, 6 + k % 2, :].rearrange("p (f x) -> p f x", f=4)).then_inc(ptr_read, 1)
                    k += 1
            xs_read(0)
            lo(4)
            for c in range(2):
                for b in range(2):
                    dve.wait_ge(ptr, k + 1)
                    for half in range(2):
                        p = slice(64 * half, 64 * half + 64)
                        src = PS[p, 6 + k % 2, :].rearrange("p (f s g h) -> p f s g h", f=4, s=SPF, g=2)[:, :, :, half, :]
                        ins = TS(CT[p, 4 * b:4 * b + 4, c], src, -1.0 if c else 1.0, None, ALU.mult)
                    ins.then_inc(ptr_read, 1)
                    k += 1
            dve.wait_ge(ptr, k + 1)
            for c in range(2):
                ins = dve.tensor_copy(init[:, c].rearrange("p s (m b) -> p m b s", m=2),
                                      PS[:, 6 + k % 2, 2 * P * c:2 * P * (c + 1)]
                                      .rearrange("p (m b s) -> p m b s", m=2, s=NST))
            ins.then_inc(ptr_read, 1)
            k += 1
            xs_read(1)
            for x in range(L.bit_length() - 1 + LVL):
                if x == 4:
                    lo(5)
                if x >= L.bit_length() - 1:
                    lv = x - (L.bit_length() - 1)
                    table(AP_[:, 2 * lv], AP_[:, 2 * lv + 1])
                m(TT(S(14), S(12), S(12), ALU.mult))
                m(TT(S(15), S(13), S(13), ALU.mult))
                m(TT(S(18), S(12), S(13), ALU.mult))
                m(TT(S(12), S(14), S(15), ALU.subtract))
                m(TS(S(13), S(18), 2.0, None, ALU.mult))
            dve.wait_ge(ptr_read, k)
            dve.nop().then_inc(s5_par, 1)
            for g in range(2, NH2):
                lo(n_xs + 2 * g + 2)
                xs_read(g)
                lo(n_xs + 2 * g + 3)

            zf = zp[:, :, :, :].rearrange("p t j h -> p t (j h)")
            for i in range(NH2):
                n = n_cv + 4 * i
                lo(n + 2)
                dve.wait_ge(unit_used, n + 2)
                dve.tensor_copy(tmp[:, :, :], PS[:, 0:2, 0:T]).then_inc(dve_read, 1)
                lo(n + 3)
                lo(n + 4)
                dve.wait_ge(unit_used, n + 4)
                TT(zf[:, 2 * i:2 * i + 2, 2 * NCH:], PS[:, 2:4, 0:T], tmp[:, :, :], ALU.mult).then_inc(dve_read, 1)
                lo(n + 5)
            dve.wait_ge(dve_read, g_xb)
            own(dve.tensor_copy(zp[:, :, 0:2, 1:NPC], zp[:, :, L:L + 2, 0:NPC - 1]))
            own(dve.memset(zp[:, :, 0:2, 0:1], 0.0))
            dve.tensor_copy(zl[:, :, :, :], zp[:, :, L:L + 2, NPC - 1:NCH]).then_inc(zl_done, 1)
            dve.wait_ge(ptr, k + 1)
            own.n += 1
            dve.tensor_copy(zp[:, :, 0:2, NPC:NCH].rearrange("p t k b -> p t b k"),
                            PS[:, 6 + k % 2, 0:2 * NB * KH].rearrange("p (t b k) -> p t b k", t=KH, k=2)).then_inc(d_in, 1)
            dve.wait_ge(d_in, own.n)
            dve.nop().then_inc(ptr_read, 1)
            k += 1

            for g in range(NH2):
                n = n_xb + 2 * g
                lo(n + 2)
                if g:
                    dve.wait_ge(th_done, g)
                    dve.wait_ge(tl_done, g)
                for m2 in range(2):
                    t = 2 * g + m2
                    wk_ = lambda kk: vecs[:, O_CW + kk * KH + t:O_CW + kk * KH + t + 1]
                    own(TS(tmp[:, m2, :], zf[:, t, 0:T], wk_(0), None, ALU.mult))
                    for kk in (1, 2):
                        own(dve.scalar_tensor_tensor(out=tmp[:, m2, :], in0=zf[:, t, kk * NCH:kk * NCH + T],
                                                     scalar=wk_(kk), in1=tmp[:, m2, :], op0=ALU.mult, op1=ALU.add))
                dve.wait_ge(unit_used, n + 2)
                b = 2 * (g % 2)
                TT(tmp[:, :, :], PS[:, b:b + 2, 0:T], tmp[:, :, :], ALU.mult).then_inc(t_done, 1)
                dve.wait_ge(t_done, g + 1)
                dve.nop().then_inc(dve_read, 1)
                if g == 0:
                    for b in range(2):
                        dve.wait_ge(ptr, k + 1)
                        dve.tensor_copy(cvrow[0:2 * (1 + NB), 512 * b:512 * (b + 1)],
                                        PS[0:2 * (1 + NB), 6 + k % 2, :]).then_inc(ptr_read, 1)
                        k += 1
                lo(n + 3)
                dve.wait_ge(th_done, g + 1)
                TT(tHL[:, 1, 2 * g:2 * g + 2, :], tmp[:, :, :], tHL[:, 0, 2 * g:2 * g + 2, :].bitcast(F32),
                   ALU.subtract).then_inc(tl_done, 1)
            dve.wait_ge(out_in, 16 * 4)
            for g in range(ND2):
                n = n_ga + 3 * g
                lo(n + 2)
                lo(n + 3)
                if g == ND2 - 1:
                    for c in range(2):
                        dve.wait_ge(yh_done, c + 1)
                        TT(gHL[:, 1, 4 * c:4 * c + 4, :], xs[:, 4 * c:4 * c + 4, :], gHL[:, 0, 4 * c:4 * c + 4, :].bitcast(F32),
                           ALU.subtract).then_inc(yl_done, 1)
                dve.wait_ge(unit_used, n + 3)
                dve.wait_ge(sig_done, g + 2)
                TT(mrg[:, 2 * g:2 * g + 2, :], PS[:, 2:4, 0:T], tmp[:, :, :], ALU.mult).then_inc(dve_read, 1)
                lo(n + 4)
            for x0, x1 in ((0, 4), (4, 6)):
                dve.wait_ge(ptr, k + 1)
                for x in range(x0, x1):
                    rows = NST if x % 3 == 0 else P
                    ins = dve.tensor_copy(frow[0:rows, x, :], PS[0:rows, 6 + k % 2, P * (x - x0):P * (x - x0 + 1)])
                ins.then_inc(ptr_read, 1)
                k += 1
            for g in range(NH2):
                lo(n_gl + g + 2)
                dve.wait_ge(sig_done, ND2 + g + 2)
                TT(xs[:, 2 * g:2 * g + 2, :], xs[:, 2 * g:2 * g + 2, :], tmp[:, :, :], ALU.mult).then_inc(gp_done, 1)
                dve.wait_ge(gh_done, g + 1)
                TT(tHL[:, 1, 2 * g:2 * g + 2, :], xs[:, 2 * g:2 * g + 2, :], tHL[:, 0, 2 * g:2 * g + 2, :].bitcast(F32),
                   ALU.subtract).then_inc(gl_done, 1)
            dve.wait_ge(wr_in, 32)
            TT(wr[:, :, :], wr[:, :, :], vecs[:, O_N2:O_N2 + KD].unsqueeze(2).to_broadcast([P, KD, NR]),
               ALU.mult).then_inc(wr_done, 1)
            dve.nop().then_inc(mg_done, 1)

            def merged_lo(c):
                dve.wait_ge(mh_done, c + 1)
                TT(uHL[:, 1, 4 * c:4 * c + 4, :], mrg[:, 4 * c:4 * c + 4, :], uHL[:, 0, 4 * c:4 * c + 4, :].bitcast(F32),
                   ALU.subtract).then_inc(ml_done, 1)

            def gb_so(i, last=False):
                for h in range(2):
                    n, g = n_gb + 6 * i + 3 * h, 2 * i + h
                    lo(n + 2)
                    lo(n + 3)
                    if last and h == 1:
                        for c in range(3):
                            merged_lo(c)
                    dve.wait_ge(unit_used, n + 3)
                    dve.wait_ge(sig_done, g + ND2 + NH2 + 2)
                    TT(tmp[:, :, :], PS[:, 2:4, 0:T], tmp[:, :, :], ALU.mult).then_inc(dve_read, 1)
                    dve.wait_ge(dve_read, g + g_ga + ND2 + 1)
                    TT(mrg[:, bass.ds(2 * g, 2), :], mrg[:, bass.ds(2 * g, 2), :], tmp[:, :, :],
                       ALU.add).then_inc(mg_done, 1)
                    if last and h == 1:
                        merged_lo(3)
                    lo(n + 4)

            with dve.Fori(0, ND2 // 2 - 1) as i:
                gb_so(i)
            gb_so(ND2 // 2 - 1, True)

            def rows_out(g):
                for m2 in range(2):
                    dve.wait_ge(hrow[m2], g + 1)
                    dve.tensor_copy(htok[0:TQ, :, bass.ds((2 * g + m2) * P, P)],
                                    PS[0:TQ, 4 + m2, :].rearrange("p (q c) -> p q c", q=Q)).then_inc(htk_done, 1)

            def w_o_group(i, h, first, last):
                g, n = 2 * i + h, n_wo + 4 * i + 2 * h
                if not last:
                    lo(n + 2)
                if not first:
                    rows_out(g - 1)
                if not last:
                    lo(n + 3)

            w_o_group(0, 0, True, False)
            w_o_group(0, 1, False, False)
            with dve.Fori(1, ND2 // 2 - 1) as i:
                w_o_group(i, 0, False, False)
                w_o_group(i, 1, False, False)
            w_o_group(ND2 // 2 - 1, 0, False, False)
            w_o_group(ND2 // 2 - 1, 1, False, True)
            rows_out(ND2 - 1)

            R = Own(dve, rdc)
            t = slice(0, TQ)
            r = lambda a, b=None: rs[t, a, :] if b is None else rs[t, a:b, :]
            bc = lambda ap, n: ap.unsqueeze(2).to_broadcast([TQ, Q, n])
            flat = lambda ap: ap.rearrange("p a q -> p (a q)")
            dve.wait_ge(cst, 5)
            for kk in range(2):
                R(TS(tk[t, 0, kk, :], toki[t, :], 1.0, None, ALU.add))
                R(TS(tk[t, 1, kk, :], toki[t, :], 2.0, 1.0 + kk, ALU.mult, ALU.add))
            dve.wait_ge(htr, ND2)
            R(dve.tensor_copy(lg[t], PS[t, 6, 0:Q * NR].rearrange("p (q n) -> p q n", q=Q)))
            R(dve.tensor_reduce(r(0), lg[t, :, 0:NEG], AX.X, ALU.max))
            R(dve.memset(cpad[t], -3.0e38))
            R(dve.tensor_copy(cpad[t, :, 0:NEG], lg[t, :, 0:NEG]))
            for q in range(Q):
                R(dve.max(m8[t, q], cpad[t, q]))
            for q in range(Q):
                R(dve.max_index(i8[t, q], m8[t, q], cpad[t, q]))
            dve.wait_ge(h_ss, 2 * Q)
            R(TT(stat[t, 0, :], stat[t, 0, :], stat[t, 4, :], ALU.add))
            TS(stat[t, 1, :], stat[t, 0, :], 1.0 / D, EPS, ALU.mult, ALU.add).then_inc(h_rs, 1)
            R(dve.tensor_copy(r(1), i8[t, :, 0]))
            iot = lambda n: iota_e[t, 0:n].unsqueeze(1).to_broadcast([TQ, Q, n])
            R(TT(oh4[t], iot(NEG), bc(r(1), NEG), ALU.is_equal))
            R(TT(lmask[t], lg[t, :, NEG:].rearrange("p q (g e) -> p q e g", g=NEG),
                 oh4[t].unsqueeze(2).to_broadcast([TQ, Q, EPG, NEG]), ALU.mult))
            R(dve.tensor_reduce(lfg[t], lmask[t], AX.X, ALU.add))
            dve.wait_ge(a_in_, Q + 1)
            R(dve.reciprocal(stat[t, 3, :], stat[t, 2, :]))
            newton(R, stat[t, 3, :], stat[t, 1, :], stat[t, 8, :]).then_inc(rn_done, 1)
            for q in range(Q):
                R(dve.max(v8[t, q], lfg[t, q]))
            for q in range(Q):
                R(dve.max_index(j8[t, q], v8[t, q], lfg[t, q]))
            R(dve.tensor_copy(r(4, 6), j8[t, :, 0:2].rearrange("p q k -> p k q")))
            R(dve.scalar_tensor_tensor(out=r(10, 12), in0=r(1).unsqueeze(1).to_broadcast([TQ, 2, Q]),
                                       scalar=float(EPG), in1=r(4, 6), op0=ALU.mult, op1=ALU.add))
            R(TT(ek[t].rearrange("p k q e -> p (k q) e"), iota_e[t, :].unsqueeze(1).to_broadcast([TQ, 2 * Q, NE]),
                 flat(r(10, 12)).unsqueeze(2).to_broadcast([TQ, 2 * Q, NE]), ALU.is_equal))
            TT(esum[t], ek[t, 0], ek[t, 1], ALU.add).then_inc(es_done, 1)
            for v in range(2):
                R(TT(etok[t, :, :, :, v].rearrange("p k q e -> p (k q) e"), ek[t].rearrange("p k q e -> p (k q) e"),
                     flat(tk[t, v]).unsqueeze(2).to_broadcast([TQ, 2 * Q, NE]), ALU.mult))
            dve.wait_ge(pos_done, 1)
            pos = PS[t, 7, 0:Q * NE].rearrange("p (q e) -> p q e", q=Q)
            for kk in range(2):
                R(TT(ep[t, kk], pos, ek[t, kk], ALU.mult))
            R(dve.tensor_reduce(flat(r(12, 14)), ep[t].rearrange("p k q e -> p (k q) e"), AX.X, ALU.add))
            TT(oc[t].rearrange("p k q c -> p (k q) c"), iota_c[t, :].unsqueeze(1).to_broadcast([TQ, 2 * Q, C]),
               flat(r(12, 14)).unsqueeze(2).to_broadcast([TQ, 2 * Q, C]), ALU.is_equal).then_inc(oc_done, 1)
            R(dve.tensor_reduce(rs[t, 18, 0:1], PS[t, 7, Q * NE:(Q + 1) * NE], AX.X, ALU.max))
            R(TS(flag[t, :], rs[t, 18, 0:1], float(C), None, ALU.is_gt))
            dve.wait_ge(slp_done, 1)
            R(TS(efar[0:C, :], PS[0:C, 6, 0:2 * NE], 0.0, float(FAR + 1), ALU.is_equal, ALU.mult))
            dve.scalar_tensor_tensor(out=slots[0:C, :, :].rearrange("p e v -> p (e v)"), in0=PS[0:C, 6, 0:2 * NE],
                                     scalar=-1.0, in1=efar[0:C, :], op0=ALU.add, op1=ALU.add).then_inc(sl_done, 1)
            R(dve.memset(r(14, 16), 0.0))
            for mm in range(1, MORE):
                R(dve.scalar_tensor_tensor(out=r(14, 16), in0=r(12, 14), scalar=float(C * mm), in1=r(14, 16),
                                           op0=ALU.is_ge, op1=ALU.add))
            R(dve.scalar_tensor_tensor(out=r(12, 14), in0=r(14, 16), scalar=-float(C), in1=r(12, 14),
                                       op0=ALU.mult, op1=ALU.add))
            R(dve.scalar_tensor_tensor(out=r(10, 12), in0=r(14, 16), scalar=float(NE), in1=r(10, 12),
                                       op0=ALU.mult, op1=ALU.add))
            R(dve.scalar_tensor_tensor(out=trow[t].rearrange("p q k -> p k q"), in0=r(12, 14), scalar=float(NITEM),
                                       in1=r(10, 12), op0=ALU.mult, op1=ALU.add))
            for kk in range(2):
                R(dve.tensor_copy(tval[t, :, kk, 0], toki[t, :]))
                R(TS(tval[t, :, kk, 1], toki[t, :], 2.0, float(kk), ALU.mult, ALU.add))
            dve.nop().then_inc(rt_done, 1)
            R(TT(cex[t], lg[t, :, 0:NEG], bc(r(0), NEG), ALU.subtract))
            TT(cex[t], cex[t], bc(stat[t, 3, :], NEG), ALU.mult).then_inc(r_arg, 1)
            R(TT(r(2), v8[t, :, 1], v8[t, :, 0], ALU.subtract))
            TT(r(2), r(2), stat[t, 3, :], ALU.mult).then_inc(r_arg, 1)
            dve.wait_ge(r_exp, 2)
            R(dve.tensor_reduce(r(6), cex[t], AX.X, ALU.add))
            R(dve.reciprocal(r(7), r(6)))
            R(TS(r(8), r(3), 1.0, None, ALU.add))
            R(dve.reciprocal(r(9), r(8)))
            R(TT(wk[t, 0, :], r(9), r(7), ALU.mult))
            R(TT(wk[t, 1, :], wk[t, 0, :], r(3), ALU.mult))
            dve.nop().then_inc(rg_done, 1)

            cursor = [0]

            def mlo_(n0, e, s):
                rr = cursor[0] % MRAW
                cursor[0] += 1
                dve.wait_ge(mhi, e * 6 + n0 + 1)
                TT(mL[s], mraw[rr], mH[s].bitcast(F32), ALU.subtract).then_inc(mlo, 1)

            def xl(e):
                for b in range(4):
                    dve.wait_ge(xh_done, e * 4 + b + 1)
                    TT(xTL[:, 4 * b:4 * b + 4, 0:C], PS[:, 2 + b % 2, 0:4 * CM].rearrange("p (k c) -> p k c", k=4)[:, :, 0:C],
                       xTH[:, 4 * b:4 * b + 4, 0:C].bitcast(F32), ALU.subtract).then_inc(xl_done, 1)

            def al(e):
                dve.wait_ge(ah_done, e + 1)
                TT(aTL[:, :, 0:C], PS[:, 1, 0:2 * CM].rearrange("p (k c) -> p k c", k=2)[:, :, 0:C],
                   aTH[:, :, 0:C].bitcast(F32), ALU.subtract).then_inc(al_done, 1)

            def am(e):
                if isinstance(e, int) and e == 0:
                    dve.wait_ge(pad_done, 5)
                dve.wait_ge(silu_done, e + 1)
                ge(dve, a_tr, e)
                TT(act_[0:C, :], PS[0:C, 0, DE:2 * DE], sg[0:C, :], ALU.mult).then_inc(am_done, 1)

            for s in range(4):
                mlo_(s, 0, s)
            xl(0)

            def body(e, first, last):
                if not first:
                    al(e - 1)
                    for h in range(2):
                        mlo_(2 + h, e, 4 + h)
                if not last:
                    for h in range(2):
                        mlo_(4 + h, e, h)
                am(e)
                if not last:
                    xl(e + 1)
                    for h in range(2):
                        mlo_(6 + h, e, 2 + h)

            body(0, True, False)
            with dve.Fori(1, NE - 1) as e:
                body(e, False, False)
            body(NE - 1, False, True)
            al(NE - 1)
            for h in range(2):
                mlo_(4 + h, NE - 1, 4 + h)

            dve.wait_ge(yo_out, 16 * NE)
            over = dve.value_load(flag[0:1, 0:1], min_val=0, max_val=1)
            with dve.If(over > 0):
                with dve.Fori(0, (MORE - 1) * NE) as n:
                    dve.wait_ge(o_si, n + 1)
                    TT(act_[0:C, :], PS[0:C, 0, DE:2 * DE], sg[0:C, :], ALU.mult).then_inc(o_am, 1)
            dve.nop()

            fc = Own(dve, fch)

            def rest(q):
                dve.wait_ge(f_ss, q + 1)
                TS(stat[t, 5, q:q + 1], stat[t, 4, q:q + 1], 1.0 / D, EPS, ALU.mult, ALU.add).then_inc(f_rs, 1)
                dve.wait_ge(f_sq, q + 1)
                fc(dve.reciprocal(stat[t, 7, q:q + 1], stat[t, 6, q:q + 1]))
                newton(fc, stat[t, 7, q:q + 1], stat[t, 5, q:q + 1], stat[t, 8, q:q + 1]).then_inc(f_rc, 1)

            for q in range(Q):
                dve.wait_ge(yk_in[q], 16)
                fc(dve.scalar_tensor_tensor(out=htok[t, q, :], in0=yk[t, q, 0, :], scalar=wk[t, 0, q:q + 1],
                                            in1=htok[t, q, :], op0=ALU.mult, op1=ALU.add))
                dve.scalar_tensor_tensor(out=htok[t, q, :], in0=yk[t, q, 1, :], scalar=wk[t, 1, q:q + 1],
                                         in1=htok[t, q, :], op0=ALU.mult, op1=ALU.add).then_inc(f_add, 1)
                if q:
                    rest(q - 1)
            rest(Q - 1)
            dve.wait_ge(f_rc, Q)
            dve.wait_ge(fn_in, 16)
            dve.scalar_tensor_tensor(out=htok[t, Q - 1, :], in0=htok[t, Q - 1, :], scalar=stat[t, 7, Q - 1:Q],
                                     in1=fnb[t, :], op0=ALU.mult, op1=ALU.mult).then_inc(f_last, 1)

        @block.gpsimd
        def _(pool):
            load_rows(pool, 3 * JQ, L, xt, x_in[3])
            pool.memset(ident[:, :], 0.0).then_inc(idn, 1)
            pool.wait_ge(idn, 1)
            pool.affine_select(out=ident[:, :], in_=ident[:, :], compare_op=ALU.not_equal, fill=1.0, base=0,
                               pattern=[[-1, P]], channel_multiplier=1).then_inc(idn, 1)
            pool.memset(ctc[:, :, :, :], 0.0).then_inc(ctz, 1)
            pool.memset(farc[:, :], FAR).then_inc(far_in, 1)
            pool.wait_ge(far_in, 1)
            pool.dma_start(tab.rearrange("(s i) v -> s (i v)", i=NITEM), farc[0:C, :]).then_inc(tab_ok, 16)

            TT = pool.tensor_tensor

            def steps(k, t1, t2, prev, a1, a2, cur):
                TT(t1, prev, a1, ALU.mult).then_inc(loc, 1)
                k.n += 1
                k(TT(t2, prev[:, ::-1], a2, ALU.mult))
                k(TT(cur, cur, t1, ALU.add))
                k(TT(cur, cur, t2, ALU.add))

            pool.wait_ge(s5_par, 1)
            with pool.Fori(0, KH // 2) as i:
                for par in range(2):
                    ft = 2 * i + par
                    f = bass.ds(ft * SPF, SPF)
                    for dst, src in zip(coef, (A1, A2)):
                        pool.tensor_copy(dst[:, :, :], src[:, :, f]).then_inc(cf_done, 1)
                    pool.tensor_copy(cpow[:, :, :, :], AP_[:, :, :, f]).then_inc(cf_done, 1)
                    pool.tensor_copy(inic[:, :, :, :], init[:, :, f, :]).then_inc(cf_done, 1)
                    fA1, fA2 = coef
                    k = Own(pool, loc, ft * (4 * (L + LVL)))
                    pool.wait_ge(cf_done, ft * 4 + 4)
                    pool.wait_ge(bu_read, ft * 8 + 8)
                    for j in range(L):
                        c0 = NPC if j == 0 else 0
                        n = NCH - c0
                        prev = inic[:, :, :, :] if j == 0 else st[:, par, j - 1, :, :, :]
                        t1, t2 = [x[:, 0:2 * SPF * n].rearrange("p (c s h) -> p c s h", c=2, s=SPF) for x in (tA, tB)]
                        a1, a2 = [x[:, :, :].unsqueeze(3).to_broadcast([P, 2, SPF, n]) for x in (fA1, fA2)]
                        steps(k, t1, t2, prev, a1, a2, st[:, par, j, :, :, c0:])
                    for lv in range(LVL):
                        n = NPC - (1 << lv)
                        t1, t2 = [x[:, 0:2 * SPF * n].rearrange("p (c s h) -> p c s h", c=2, s=SPF) for x in (tA, tB)]
                        a1, a2 = [cpow[:, 2 * lv + x, :, :].unsqueeze(3).to_broadcast([P, 2, SPF, n]) for x in (0, 1)]
                        steps(k, t1, t2, st[:, par, L - 1, :, :, 0:n], a1, a2, st[:, par, L - 1, :, :, 1 << lv:NPC])
                    pool.nop().then_inc(loc_done, 1)

            pool.wait_ge(gl_done, NH2)
            load_rows(pool, 0, L, xt2, xt2_in)

            pool.wait_ge(g2_in, 16)
            for g in range(ND2):
                if g == ND2 - 1:
                    pool.wait_ge(res_done, ND2)
                    pool.memset(one[:, :], 1.0).then_inc(cst, 1)
                    pool.iota(iota_e[:, :], pattern=[[1, NE]], base=0, channel_multiplier=0,
                              allow_small_or_imprecise_dtypes=True).then_inc(cst, 1)
                    pool.iota(toki[:, :], pattern=[[TQ, Q]], base=0, channel_multiplier=1,
                              allow_small_or_imprecise_dtypes=True).then_inc(cst, 1)
                    pool.iota(iota_c[:, :], pattern=[[1, C]], base=0, channel_multiplier=0,
                              allow_small_or_imprecise_dtypes=True).then_inc(cst, 1)
                    pool.wait_ge(cst, 4)
                    pool.affine_select(out=lst[:, :], in_=one[:, :], compare_op=ALU.is_gt, fill=0.0, base=0,
                                       pattern=[[1, P]], channel_multiplier=-1).then_inc(cst, 1)
                c = slice(g * UW, (g + 1) * UW)
                pool.wait_ge(htk_done, 2 * g + 2)
                pool.wait_ge(xst_done, g + 1)
                TT(xt2[0:TQ, :, c], htok[0:TQ, :, c], g2b[0:TQ, c].unsqueeze(1).to_broadcast([TQ, Q, UW]),
                   ALU.mult).then_inc(g_done, 1)

            pool.wait_ge(htr, ND2)
            for x in (xTH, xTL, aTH, aTL):
                pool.memset(x[:, :, C:].bitcast(F32), 0.0).then_inc(pad_done, 1)
            pool.memset(act_[:, :], 0.0).then_inc(pad_done, 1)
            pool.wait_ge(g_done, ND2)
            pool.memset(xg[:, :], 0.0).then_inc(xgz, 1)

            def gather(s):
                pool.nop().then_inc(pl, 1)
                pool.indirect_dma_start(out=xg[0:C, :], out_offset=None, in_=vbuf[:, :],
                                        in_offset=bass.IndirectOffsetOnAxis(ap=idg[0:C, 0:1], axis=0),
                                        bounds_check=T - 1, oob_is_err=False).then_inc(s, 16)

            def scatter(s):
                pool.nop().then_inc(pl, 1)
                pool.indirect_dma_start(out=ybuf[:, :],
                                        out_offset=bass.IndirectOffsetOnAxis(ap=ids[0:C, 1:2], axis=0),
                                        in_=yo[0:C, :], in_offset=None, bounds_check=2 * T - 1,
                                        oob_is_err=False).then_inc(s, 16)

            def gather_e(e):
                ge(pool, xg_in, e * 16)
                pool.tensor_copy(idg[0:C, :], slots[0:C, e, :]).then_inc(ix_done, 1)
                pool.wait_ge(ix_done, e + 1)
                ge(pool, xg_tr, e * 4)
                gather(xg_in)

            def scatter_e(e):
                ge(pool, yo_out, e * 16)
                pool.tensor_copy(ids[0:C, :], slots[0:C, e, :]).then_inc(pst, 1)
                pool.wait_ge(pst, e + 1)
                pool.wait_ge(yo_done, e + 1)
                scatter(yo_out)

            pool.wait_ge(xgz, 1)
            pool.wait_ge(sl_done, 1)
            pool.wait_ge(v_out, 16 * Q)
            gather_e(0)
            pool.wait_ge(tab_ok, 16)
            pool.wait_ge(rt_done, 1)
            for q in range(Q):
                for kk in range(2):
                    pool.indirect_dma_start(
                        out=tab[:, :], out_offset=bass.IndirectOffsetOnAxis(ap=trow[0:TQ, q, kk:kk + 1], axis=0),
                        in_=tval[0:TQ, q, kk, :], in_offset=None, bounds_check=C * NITEM - 1,
                        oob_is_err=False).then_inc(sc_out[2 * q + kk], 16)
            gather_e(1)
            gather_e(2)
            with pool.Fori(2, NE - 1) as e:
                gather_e(e + 1)
                scatter_e(e - 2)
            for e in range(NE - 3, NE):
                scatter_e(e)

            pool.wait_ge(yo_out, 16 * NE)
            over = pool.value_load(flag[0:1, 0:1], min_val=0, max_val=1)
            with pool.If(over > 0):
                pool.wait_ge(osl_in, 16)
                with pool.Fori(0, (MORE - 1) * NE) as n:
                    pool.tensor_copy(idg[0:C, :], oslots[0:C, n + NE, :]).then_inc(o_ix, 1)
                    pool.tensor_copy(ids[0:C, :], oslots[0:C, n + NE, :]).then_inc(o_ix, 1)
                    pool.wait_ge(o_ix, n * 2 + 2)
                    gather(o_x)
                    pool.wait_ge(o_ye, n + 2)
                    scatter(o_y)
                    pool.wait_ge(o_y, n * 16 + 16)
            pool.nop()

            pool.wait_ge(fn_in, 16)
            for q in range(Q - 1):
                pool.wait_ge(f_nrm, q + 1)
                TT(htok[0:TQ, q, :], htok[0:TQ, q, :], fnb[0:TQ, :], ALU.mult).then_inc(f_out, 1)


_INS = ["x_prompt", "x_sample", "state_conv", "state_ssm_re", "state_ssm_im", "meta_tokens", "norm1", "w_in",
        "conv_w", "lam_re", "lam_im", "log_dt", "ssm_b_re", "ssm_b_im", "ssm_c_re", "ssm_c_im", "ssm_d", "w_glu",
        "w_conv_out", "w_ssm_out", "w_o", "norm2", "w_coarse", "w_fine", "w_gate", "w_up", "w_down", "final_norm"]


def program(nc, inputs):
    ins = [nc.dram_tensor(n, inputs[n].shape, F32, kind="ExternalInput").ap() for n in _INS]
    xp, xsm, sc, sr = (inputs[n].shape for n in ("x_prompt", "x_sample", "state_conv", "state_ssm_re"))
    shapes = [xp, xsm, (sc[0], xp[0]) + tuple(sc[2:]), (sr[0], xp[0]) + tuple(sr[2:]),
              (sr[0], xp[0]) + tuple(sr[2:]), sc, sr, sr]
    outs = [nc.dram_tensor(f"out_{i}", tuple(s), F32, kind="ExternalOutput").ap() for i, s in enumerate(shapes)]
    build(nc, ins, outs)
    return [f"out_{i}" for i in range(len(outs))]


def kernel(**inputs):
    import concourse.bacc as bacc
    import numpy as np
    from concourse.bass_utils import run_bass_kernel_spmd

    arrays = {n: np.ascontiguousarray(inputs[n]) for n in _INS}
    nc = bacc.Bacc("TRN2", target_bir_lowering=False, num_devices=1, dynamic_dma_scratch_size=2048)
    names = program(nc, arrays)
    r = run_bass_kernel_spmd(nc, [arrays], core_ids=[0])
    return tuple(r.results[0][n] for n in names)
```
